# Optimizing a Trainium2 kernel written in Bass

```python
import math
import jax, jax.numpy as jnp
from jax import lax
import numpy as np

D_MODEL = 1024
BATCH = 1
SEQ = 1024
DEPTH = 2

GLA_HEADS = 4
GLA_DV = D_MODEL // 8
GLA_DK = GLA_DV // 2
GLA_LOWRANK = 16
GLA_TAU = 16.0
GLA_CHUNK = 64
DIFF_HEADS = 4
DIFF_DV = D_MODEL // 8
DIFF_DQK = DIFF_DV // 2
Q_BLOCK = 128
REL_BUCKETS = 32
REL_MAX_DIST = 128
MIX_WIDTH = GLA_HEADS * GLA_DV + DIFF_HEADS * DIFF_DV
D_FF = -(-8 * D_MODEL // (3 * 256)) * 256
RMS_EPS = 1e-6

IN_SIZES = [
    GLA_HEADS * GLA_DK,
    GLA_HEADS * GLA_DK,
    GLA_HEADS * GLA_DV,
    GLA_HEADS * GLA_DV,
    GLA_LOWRANK,
    DIFF_HEADS * 2 * DIFF_DQK,
    DIFF_HEADS * 2 * DIFF_DQK,
    DIFF_HEADS * DIFF_DV,
]
IN_WIDTH = sum(IN_SIZES)
IN_SPLITS = [int(s) for s in np.cumsum(IN_SIZES)[:-1]]

kernel_name = "hymba_gla_diffattn_t5bias_sandwich_adaln"

def rms_norm(x, g):
    xf = x.astype(jnp.float32)
    y = xf * lax.rsqrt(jnp.mean(xf * xf, axis=-1, keepdims=True) + RMS_EPS)
    return (y * g.astype(jnp.float32)).astype(x.dtype)

def t5_bucket(rel):
    max_exact = REL_BUCKETS // 2
    n = jnp.maximum(rel, 0)
    nf = jnp.maximum(n, 1).astype(jnp.float32)
    large = max_exact + (jnp.log(nf / max_exact) / math.log(REL_MAX_DIST / max_exact)
                         * (REL_BUCKETS - max_exact)).astype(jnp.int32)
    large = jnp.minimum(large, REL_BUCKETS - 1)
    return jnp.where(n < max_exact, n, large)

def gla_chunked(q, k, v, log_a):
    B, S, H, dk = q.shape
    dv = v.shape[-1]
    C = GLA_CHUNK
    N = S // C

    def blk(t):
        return t.astype(jnp.float32).reshape(B, N, C, H, t.shape[-1]).transpose(0, 3, 1, 2, 4)

    q, k, v, log_a = blk(q) * (dk ** -0.5), blk(k), blk(v), blk(log_a)
    b = jnp.cumsum(log_a, axis=3)
    b_last = b[:, :, :, -1:, :]
    q_e = q * jnp.exp(b)
    k_e = k * jnp.exp(-b)
    causal = jnp.tril(jnp.ones((C, C), dtype=bool))
    a_intra = jnp.where(causal, jnp.einsum('bhncd,bhnjd->bhncj', q_e, k_e), 0.0)
    o_intra = jnp.einsum('bhncj,bhnjv->bhncv', a_intra, v)
    u = jnp.einsum('bhncd,bhncv->bhndv', k * jnp.exp(b_last - b), v)
    decay = jnp.exp(b_last[:, :, :, 0, :])

    def step(state, inp):
        u_n, d_n = inp
        return d_n[..., None] * state + u_n, state

    _, s_prev = lax.scan(step, jnp.zeros((B, H, dk, dv), jnp.float32),
                         (jnp.moveaxis(u, 2, 0), jnp.moveaxis(decay, 2, 0)))
    s_prev = jnp.moveaxis(s_prev, 0, 2)
    o = o_intra + jnp.einsum('bhncd,bhndv->bhncv', q_e, s_prev)
    return o.transpose(0, 2, 3, 1, 4).reshape(B, S, H, dv)

def diff_attention(q, k, v, rel_bias, lam):
    S = q.shape[1]
    scale = DIFF_DQK ** -0.5
    bias_tab = rel_bias.astype(jnp.float32)
    outs = []
    for i in range(S // Q_BLOCK):
        q0 = i * Q_BLOCK
        end = q0 + Q_BLOCK
        s = jnp.einsum('bqhmd,bkhmd->bhmqk', q[:, q0:end], k[:, :end]).astype(jnp.float32) * scale
        rel = jnp.arange(q0, end)[:, None] - jnp.arange(end)[None, :]
        bias = jnp.transpose(bias_tab[t5_bucket(rel)], (2, 0, 1))
        s = s + bias[None, :, None]
        s = jnp.where(rel >= 0, s, -jnp.inf)
        p = jax.nn.softmax(s, axis=-1)
        a = p[:, :, 0] - lam * p[:, :, 1]
        outs.append(jnp.einsum('bhqk,bkhv->bqhv', a.astype(v.dtype), v[:, :end]))
    return jnp.concatenate(outs, axis=1)

def token_mixer(h, w_in, w_gla_gate, b_gla_gate, gla_norm, diff_lambda, diff_norm,
                rel_bias, w_out, lam_init):
    B, S, _ = h.shape
    proj = h @ w_in
    gq, gk, gv, gr, ga, dq, dk, dv = jnp.split(proj, IN_SPLITS, axis=-1)
    log_a = jax.nn.log_sigmoid((ga @ w_gla_gate + b_gla_gate).astype(jnp.float32)) / GLA_TAU
    o_g = gla_chunked(gq.reshape(B, S, GLA_HEADS, GLA_DK), gk.reshape(B, S, GLA_HEADS, GLA_DK),
                      gv.reshape(B, S, GLA_HEADS, GLA_DV), log_a.reshape(B, S, GLA_HEADS, GLA_DK))
    o_g = rms_norm(o_g, gla_norm) * jax.nn.silu(gr.reshape(B, S, GLA_HEADS, GLA_DV).astype(jnp.float32))
    lf = diff_lambda.astype(jnp.float32)
    lam = jnp.exp(jnp.sum(lf[0] * lf[1])) - jnp.exp(jnp.sum(lf[2] * lf[3])) + lam_init
    o_d = diff_attention(dq.reshape(B, S, DIFF_HEADS, 2, DIFF_DQK), dk.reshape(B, S, DIFF_HEADS, 2, DIFF_DQK),
                         dv.reshape(B, S, DIFF_HEADS, DIFF_DV), rel_bias, lam)
    o_d = rms_norm(o_d.astype(jnp.float32), diff_norm) * (1.0 - lam_init)
    o = jnp.concatenate([o_g.reshape(B, S, -1), o_d.reshape(B, S, -1)], axis=-1).astype(h.dtype)
    return o @ w_out

def swiglu(h, w_gate_up, w_down):
    gate, up = jnp.split(h @ w_gate_up, 2, axis=-1)
    return (jax.nn.silu(gate) * up) @ w_down

def setup_inputs(seed: int = 0) -> dict:
    key = jax.random.key(seed)
    ks = jax.random.split(key, 16)
    f32 = jnp.float32
    nrm = lambda k, shape, s: jax.random.normal(k, shape, f32) * s
    return {
        "x": nrm(ks[0], (BATCH, SEQ, D_MODEL), 1.0),
        "c": nrm(ks[1], (BATCH, D_MODEL), 1.0),
        "w_mod": nrm(ks[2], (DEPTH, D_MODEL, 6 * D_MODEL), 0.5 * D_MODEL ** -0.5),
        "b_mod": nrm(ks[3], (DEPTH, 6 * D_MODEL), 0.02),
        "norm_gains": 1.0 + nrm(ks[4], (DEPTH, 4, D_MODEL), 0.05),
        "w_in": nrm(ks[5], (DEPTH, D_MODEL, IN_WIDTH), D_MODEL ** -0.5),
        "w_gla_gate": nrm(ks[6], (DEPTH, GLA_LOWRANK, GLA_HEADS * GLA_DK), GLA_LOWRANK ** -0.5),
        "b_gla_gate": nrm(ks[7], (DEPTH, GLA_HEADS * GLA_DK), 0.1),
        "gla_norm": 1.0 + nrm(ks[8], (DEPTH, GLA_DV), 0.05),
        "diff_lambda": nrm(ks[9], (DEPTH, 4, DIFF_DQK), 0.1),
        "diff_norm": 1.0 + nrm(ks[10], (DEPTH, DIFF_DV), 0.05),
        "rel_bias": nrm(ks[11], (REL_BUCKETS, DIFF_HEADS), 0.5),
        "w_out": nrm(ks[12], (DEPTH, MIX_WIDTH, D_MODEL), MIX_WIDTH ** -0.5),
        "w_gate_up": nrm(ks[13], (DEPTH, D_MODEL, 2 * D_FF), D_MODEL ** -0.5),
        "w_down": nrm(ks[14], (DEPTH, D_FF, D_MODEL), D_FF ** -0.5),
    }

def reference(x, c, w_mod, b_mod, norm_gains, w_in, w_gla_gate, b_gla_gate, gla_norm,
              diff_lambda, diff_norm, rel_bias, w_out, w_gate_up, w_down):
    cond = jax.nn.silu(c)
    for l in range(DEPTH):
        lam_init = 0.8 - 0.6 * math.exp(-0.3 * l)
        mod = (cond @ w_mod[l] + b_mod[l])[:, None, :]
        sh1, sc1, g1, sh2, sc2, g2 = jnp.split(mod, 6, axis=-1)
        h = rms_norm(x, norm_gains[l, 0]) * (1.0 + sc1) + sh1
        y = token_mixer(h, w_in[l], w_gla_gate[l], b_gla_gate[l], gla_norm[l], diff_lambda[l],
                        diff_norm[l], rel_bias, w_out[l], lam_init)
        x = x + g1 * rms_norm(y, norm_gains[l, 1])
        h = rms_norm(x, norm_gains[l, 2]) * (1.0 + sc2) + sh2
        y = swiglu(h, w_gate_up[l], w_down[l])
        x = x + g2 * rms_norm(y, norm_gains[l, 3])
    return x


_drawn_inputs = setup_inputs


def setup_inputs(seed=0):
    import zlib

    import numpy as np

    out = dict(_drawn_inputs(seed))
    spreads = {}
    factors = {'b_gla_gate': 3.736, 'gla_norm': 4.142, 'diff_lambda': 4.811, 'diff_norm': 3.144}
    for name, (base, spread) in spreads.items():
        noise = np.random.default_rng([zlib.crc32(name.encode()), seed]).standard_normal(out[name].shape)
        drawn = base * np.exp(spread * noise) if base else spread * noise
        out[name] = __import__('jax').numpy.asarray(drawn.astype(out[name].dtype))
    for name, factor in factors.items():
        out[name] = (out[name] * factor).astype(out[name].dtype)
    return out
```

```python
import math

import numpy as np

import concourse.bass as bass
from concourse import mybir
from contextlib import ExitStack

F32 = mybir.dt.float32
F32R = mybir.dt.float32r
ACT = mybir.ActivationFunctionType
ALU = mybir.AluOpType
AX = mybir.AxisListType

D = 1024
S = 1024
L = 2
P = 128
KT = D // P
NT = S // P
HALF = 512
LOW = 16
DK = 64
DV = 128
CH = 64
HEADS = 4
FF = -(-8 * D // (3 * 256)) * 256
JT = FF // P
W_IN = 3088
C_GQ, C_GK, C_GV, C_GR, C_GA, C_DQ, C_DV = 0, 256, 512, 1024, 1536, 1552, 2576
EPS = 1e-6
BUCKETS, MAX_DIST = 32, 128
MASKED = -3.0e38
NEAR = 2 * P

N_GA, N_GK0, N_WG, N_GK1, N_GQ0, N_GQ1 = range(6)
N_GV = 6
N_GR = N_GV + 4
N_DQK = N_GR + 4
N_DV = N_DQK + 8
N_OUT = N_DV + 4
N_FF = N_OUT + 2 * KT
N_DOWN = N_FF + 2 * JT
SLOTS = N_DOWN + 2 * JT
MODS = 6 * KT
SLOT = KT * P
assert SLOTS % 2 == 0

P_A, P_B, P_G = 0, 8, 16
P_GN, P_DN, P_LAM, P_BG, NPAR = 48, 49, 50, 51, 53

C_ID, C_MASK, C_LAM = 0, P, 2 * P
NCONST = 2 * P + 2 * L
NROW = 2 * (KT * 4) + 2 * L


def layer_constants():
    c = np.zeros((P, NCONST), np.float32)
    j, q = np.arange(P)[:, None], np.arange(P)[None, :]
    c[:, C_ID:C_ID + P] = j == q
    c[:, C_MASK:C_MASK + P] = (j <= q) & (j // CH == q // CH)
    for l in range(L):
        lam = 0.8 - 0.6 * math.exp(-0.3 * l)
        c[:, C_LAM + 2 * l] = lam
        c[:, C_LAM + 2 * l + 1] = 1.0 - lam
    exact = BUCKETS // 2
    hot = np.zeros((BUCKETS + 1, 3 * P), np.float32)
    for at in range(3 * P - 1):
        d = 2 * P - 1 - at
        n = max(d, 0)
        b = n if n < exact else min(BUCKETS - 1, exact + int(
            np.float32(np.log(np.float32(n) / np.float32(exact)))
            / np.float32(math.log(MAX_DIST / exact)) * np.float32(BUCKETS - exact)))
        hot[b, at] += 1.0
        hot[BUCKETS - 1, at] -= 1.0
        if d < 0:
            hot[BUCKETS, at] = 1.0
    return c, hot


def build(nc, x, c, w_mod, b_mod, gains, w_in, w_gate, b_gate, gla_norm, lam_w, diff_norm,
          rel_bias, w_out, w_gu, w_down, consts, onehot, skew, out):
    ctx = ExitStack()
    with ctx:
        def sb(name, shape, dt=F32):
            return ctx.enter_context(nc.sbuf_tensor(name, shape, dt))

        def sem(name):
            return ctx.enter_context(nc.semaphore(name))

        hT = sb("hT", [P, 2, KT, S], F32R)
        wsp = sb("wsp", [P, 2, 2, SLOT], F32R)
        raw = sb("raw", [P, 2, SLOT])
        F = sb("F", [P, JT * S])
        W = sb("W", [P, 5 * 1024])
        cst = sb("cst", [P, NCONST])
        ones = sb("ones", [P, P])
        par = sb("par", [P, L, NPAR])
        cur = sb("cur", [P, NPAR])
        gaT = sb("gaT", [LOW, 2, S], F32R)
        cond = sb("cond", [P, KT])
        mhalf = sb("mhalf", [P, 16])
        st = sb("st", [P, 96])
        ast = sb("ast", [P, 112])
        ps = ctx.enter_context(nc.psum_tensor("ps", [P, 8, 512], F32))
        ident = cst[:, C_ID:C_ID + P]
        gmask = cst[:, C_MASK:C_MASK + P]

        Fq, Fk, Fv, Fg, Fgq, Fgk, Flg = 0, 4096, 8192, 12288, 16384, 18432, 20480
        Fp, Fat, Fbias = 16384, 20480, 21504
        Fx, Fxn, Fv4, Fj = 0, 8192, 16384, 20480
        gb = W[:, 0:1024]
        xt = [W[:, 1024:2048], W[:, 2048:3072]]
        wt = [W[:, 3072:4096], W[:, 4096:5120]]
        diag = W[:, 4096:5120].rearrange("p (k n) -> p k n", k=KT)
        Wd = W[:, 0:256]
        We = [W[:, 256 + 256 * i:512 + 256 * i] for i in range(3)]
        Wvt = W[:, 512:1024]
        Wqe = [[W[:, 1024 + 512 * r + 256 * z:1280 + 512 * r + 256 * z] for z in range(2)]
               for r in range(2)]
        Wke = [W[:, 2048:2304], W[:, 2304:2560]]
        Wkd = [W[:, 2560:2816], W[:, 2816:3072]]
        Wkn = [W[:, 3072:3328], W[:, 3328:3584]]
        Wam = W[:, 3584:4096]
        Wsq = Wam
        Ws = [W[:, 4096 + 256 * i:4352 + 256 * i] for i in range(4)]
        Wq, Won, Wv, Wj = [W[:, 0:1024], W[:, 4096:5120]], W[:, 1024:2048], W[:, 2048:3072], W[:, 3072:3200]
        S_SS, S_MS, S_RS = 0, 24, 48
        S_GSS, S_GMS, S_GRS = 72, 76, 80
        A_MX, A_NM, A_R, A_RI, A_CO, A_SS, A_M1, A_MS, A_RS = 0, 16, 32, 48, 64, 72, 80, 88, 96

        s_cst, s_small, s_ones, s_mh = sem("s_cst"), sem("s_small"), sem("s_ones"), sem("s_mh")
        s_xcopy = sem("s_xcopy")
        s_raw = [sem("s_raw0"), sem("s_raw1")]
        s_hi, s_lo = sem("s_hi"), sem("s_lo")
        s_pe = sem("s_pe")
        s_rows, s_cols, s_cond = sem("s_rows"), sem("s_cols"), sem("s_cond")
        s_mod, s_modv, s_par = sem("s_mod"), sem("s_modv"), sem("s_par")
        s_lp, s_lr, s_le = sem("s_lp"), sem("s_lr"), sem("s_le")
        s_rx, s_rb, s_rbs, s_skew = sem("s_rx"), sem("s_rb"), sem("s_rbs"), sem("s_skew")
        s_cur = sem("s_cur")
        s_bias = sem("s_bias")
        s_xl = [sem(f"s_xl{i}") for i in range(4)]
        s_xr = [sem("s_xr0"), sem("s_xr1")]
        s_n1ss, s_n1ms, s_n1rs = sem("s_n1ss"), sem("s_n1ms"), sem("s_n1rs")
        s_yss, s_yms, s_yrs = sem("s_yss"), sem("s_yms"), sem("s_yrs")
        s_n2ss, s_n2ms, s_n2rs = sem("s_n2ss"), sem("s_n2ms"), sem("s_n2rs")
        s_y, s_yu = sem("s_y"), sem("s_yu")
        s_xs = sem("s_xs")
        s_st = [sem("s_st0"), sem("s_st1")]
        s_xn, s_tr, s_v = sem("s_xn"), sem("s_tr"), sem("s_v")
        s_hh, s_hl = sem("s_hh"), sem("s_hl")
        s_gah, s_gal = sem("s_gah"), sem("s_gal")
        s_zb, s_ab, s_ez, s_ln = sem("s_zb"), sem("s_ab"), sem("s_ez"), sem("s_ln")
        s_lg = sem("s_lg")
        s_tev = sem("s_tev")
        s_nt = sem("s_nt")
        s_gv, s_gr, s_dv = sem("s_gv"), sem("s_gr"), sem("s_dv")
        s_gz = sem("s_gz")
        s_gs0 = sem("s_gs0")
        s_gsc, s_gD, s_gE, s_gC = sem("s_gsc"), sem("s_gD"), sem("s_gE"), sem("s_gC")
        s_gA, s_gd, s_gU, s_gS = sem("s_gA"), sem("s_gd"), sem("s_gU"), sem("s_gS")
        s_gO, s_gsq, s_gss, s_gms = sem("s_gO"), sem("s_gsq"), sem("s_gss"), sem("s_gms")
        s_grs, s_gG, s_gvt = sem("s_grs"), sem("s_gG"), sem("s_gvt")
        s_oT, s_ov = sem("s_oT"), sem("s_ov")
        s_oh, s_ol = sem("s_oh"), sem("s_ol")
        s_qz = sem("s_qz")
        s_q, s_qk, s_ba, s_mr, s_mx = sem("s_q"), sem("s_qk"), sem("s_ba"), sem("s_mr"), sem("s_mx")
        s_ex, s_rc, s_co, s_ad = sem("s_ex"), sem("s_rc"), sem("s_co"), sem("s_ad")
        s_at, s_ate, s_pv = sem("s_at"), sem("s_ate"), sem("s_pv")
        s_asq, s_am1, s_ams, s_ars, s_on = sem("s_asq"), sem("s_am1"), sem("s_ams"), sem("s_ars"), sem("s_on")
        s_dg, s_gbp, s_gb = sem("s_dg"), sem("s_gbp"), sem("s_gb")
        s_yt = sem("s_yt")
        s_f1, s_f2 = sem("s_f1"), sem("s_f2")
        s_ah, s_al = sem("s_ah"), sem("s_al")
        block = ctx.enter_context(nc.Block())

        CREDIT = 2

        def raw_in(l, n):
            return l * (8 * SLOTS) + 16 * (L * MODS // 2 + n // 2 + 1)

        def kn(a):
            return a.rearrange("p (k n) -> p k n", k=KT)

        def tile_of_pairs(base, i, r):
            return F[:, base:base + 2 * S].rearrange("p (a n) -> p a n", a=2)[
                :, :, bass.ds(i * (2 * P) + r * P, P)]

        def head_of_hT(m, h):
            return hT[:, m].rearrange("p k s -> p (k s)")[:, bass.ds(h * S, S)]

        xv = out.rearrange("(t p) d -> p t d", p=P)

        def apart(eng):
            eng.nop(nofuse=True)

        @block.sync
        def _(sp):
            sp.dma_start(cst[:], consts).then_inc(s_cst, 16)
            at = 0
            for src in (gains.rearrange("l i (k p) -> (l i k) p", p=P), gla_norm, diff_norm,
                        b_gate.rearrange("l (k p) -> (l k) p", p=P),
                        c.rearrange("b (k p) -> (b k) p", p=P)):
                n = src.shape[0]
                sp.dma_start(F[at:at + n, 0:P], src).then_inc(s_small, 16)
                at += n
            sp.dma_start(F[0:L * MODS, P:2 * P],
                         b_mod.rearrange("l (k p) -> (l k) p", p=P)).then_inc(s_small, 16)
            sp.dma_start(F[:, 256:256 + L * 4 * DK],
                         lam_w.rearrange("l i d -> (l i d)")[None, :].to_broadcast([P, L * 4 * DK])
                         ).then_inc(s_small, 16)
            sp.dma_start(F[0:BUCKETS, 768:768 + HEADS], rel_bias).then_inc(s_small, 16)
            sp.dma_start(F[0:BUCKETS + 1, 1024:1024 + 3 * P], onehot).then_inc(s_small, 16)
            mods = w_mod.rearrange("l (k p) c -> p l k c", p=P)
            with sp.Fori(0, L) as l:
                with sp.Fori(0, MODS // 2) as j:
                    for r in range(2):
                        sp.wait_ge(s_mod, l * MODS + j * 2 + r + 1)
                        sp.dma_start(kn(raw[:, r, :]),
                                     mods[:, l, :, bass.ds(j * (2 * P) + r * P, P)]
                                     ).then_inc(s_raw[r], 16)
            sp.wait_ge(s_mod, L * MODS + CREDIT)

            sp.wait_ge(s_rbs, HEADS)
            sp.dma_start(skew.rearrange("h q j -> q h j"),
                         F[:, 2048:2048 + HEADS * 3 * P].rearrange("p (h j) -> p h j", h=HEADS)
                         ).then_inc(s_skew, 16)

            win = w_in.rearrange("l (k p) c -> p l k c", p=P)
            wo = w_out.rearrange("l (k p) c -> p l k c", p=P)
            wgu = w_gu.rearrange("l (k p) c -> p l k c", p=P)
            wdn = w_down.rearrange("l (k p) c -> p l k c", p=P)
            with sp.Fori(0, L) as l:
                def load(g, r, dst, src):
                    sp.wait_ge(s_lo, g + 1)
                    apart(sp)
                    sp.dma_start(dst, src).then_inc(s_raw[r], 16)

                def columns(n, c0, w=P):
                    r = n % 2
                    load(l * SLOTS + n, r,
                         raw[:, r, 0:KT * w].rearrange("p (k n) -> p k n", k=KT),
                         win[:, l, :, bass.ds(c0, w)])

                columns(N_GA, C_GA, LOW)
                columns(N_GK0, C_GK)
                load(l * SLOTS + N_WG, 0, raw[0:LOW, 0, 0:256], w_gate[l])
                columns(N_GK1, C_GK + P)
                columns(N_GQ0, C_GQ)
                columns(N_GQ1, C_GQ + P)

                def rows4(n0, c0):
                    for i in range(4):
                        n = n0 + i
                        load(l * SLOTS + n, n % 2,
                             raw[:, n % 2, :].rearrange("p (k n) -> p k n", k=2),
                             win[:, l, 2 * i:2 * i + 2, c0:c0 + 512])
                rows4(N_GV, C_GV)
                rows4(N_GR, C_GR)
                with sp.Fori(0, 4) as i:
                    for r in range(2):
                        load(l * SLOTS + i * 2 + (N_DQK + r), r, kn(raw[:, r, :]),
                             win[:, l, :, bass.ds(i * (2 * P) + (C_DQ + r * P), P)])
                rows4(N_DV, C_DV)
                for g in range(2):
                    with sp.Fori(0, KT // 2) as i:
                        for r in range(2):
                            load(l * SLOTS + i * 2 + (N_OUT + g * KT + r), r, raw[:, r, :],
                                 wo[:, l, i * 2 + r, :])
                with sp.Fori(0, JT) as j:
                    for r in range(2):
                        load(l * SLOTS + j * 2 + (N_FF + r), r, kn(raw[:, r, :]),
                             wgu[:, l, :, bass.ds(j * P + r * FF, P)])
                for g in range(2):
                    with sp.Fori(0, JT // 2) as i:
                        for r in range(2):
                            load(l * SLOTS + i * 2 + (N_DOWN + g * JT + r), r, raw[:, r, :],
                                 wdn[:, l, i * 2 + r, :])

        @block.gpsimd
        def _(pool):
            pool.dma_start(out, x).then_inc(s_xcopy, 16)
            nc.gpsimd.memset(mhalf[:], -0.5).then_inc(s_mh, 1)
            pool.wait_ge(s_mh, 1)
            pool.wait_ge(s_xcopy, 16)
            pool.wait_ge(s_par, 1)
            pool.wait_ge(s_skew, 16)

            def rsqrt(into, frm, w, done):
                nc.gpsimd.tensor_tensor(st[:, into:into + w], st[:, frm:frm + w],
                                        mhalf[:, 0:w], ALU.pow).then_inc(done, 1)

            def load_x():
                for i in range(4):
                    apart(pool)
                    pool.dma_start(F[:, 2048 * i:2048 * i + 2048].rearrange("p (t d) -> p t d", t=2),
                                   xv[:, 2 * i:2 * i + 2, :]).then_inc(s_xl[i], 16)

            def new_x(l, t):
                pool.wait_ge(s_xs, l * 16 + t + 1)
                apart(pool)
                pool.dma_start(xv[:, t, :], F[:, Fx + D * t:Fx + D * t + D]).then_inc(s_st[t % 2], 16)
                pool.wait_ge(s_n2ms, l * 8 + t + 1)
                rsqrt(S_RS + 16 + t, S_MS + 16 + t, 1, s_n2rs)

            with pool.Fori(0, L) as l:
                pool.wait_ge(s_al, 1 + l * (2 * JT))
                load_x()
                pool.wait_ge(s_n1ms, l + 1)
                rsqrt(S_RS, S_MS, 8, s_n1rs)
                with pool.Fori(0, NT) as t:
                    pool.wait_ge(s_gms, l * NT + t + 1)
                    rsqrt(S_GRS, S_GMS, HEADS, s_grs)
                pool.wait_ge(s_gC, l * NT + NT)
                src = bass.AP(tensor=skew.tensor, offset=skew.offset + P - 1,
                              ap=[[3 * P - 1, P], [P * 3 * P, HEADS], [1, NEAR]])
                apart(pool)
                pool.dma_start(F[:, Fbias:Fbias + HEADS * NEAR].rearrange("p (h k) -> p h k", h=HEADS),
                               src).then_inc(s_bias, 16)
                with pool.Fori(0, HEADS) as h:
                    for b in range(NT):
                        pool.wait_ge(s_ams, l * (HEADS * NT) + h * NT + (b + 1))
                        nc.gpsimd.tensor_tensor(ast[:, A_RS + b:A_RS + b + 1],
                                                ast[:, A_MS + b:A_MS + b + 1],
                                                mhalf[:, 0:1], ALU.pow).then_inc(s_ars, 1)
                pool.wait_ge(s_qk, 1 + l * 64 + 64)
                pool.wait_ge(s_q, l * HEADS + HEADS)
                load_x()
                for g in range(2):
                    for i in range(4):
                        t = 4 * g + i
                        pool.wait_ge(s_yms, l * 16 + t + 1)
                        rsqrt(S_RS + 8 + t, S_MS + 8 + t, 1, s_yrs)
                        if i:
                            new_x(l, t - 1)
                    new_x(l, 4 * g + 3)
                pool.wait_ge(s_f2, l * JT + JT + CREDIT)
                for t in range(2):
                    apart(pool)
                    pool.dma_start(xt[t], xv[:, t, :]).then_inc(s_xr[t], 16)
                for t in range(NT):
                    pool.wait_ge(s_yms, l * 16 + 8 + t + 1)
                    rsqrt(S_RS + 8 + t, S_MS + 8 + t, 1, s_yrs)
                    if 1 <= t < NT - 1:
                        r = (t - 1) % 2
                        pool.wait_ge(s_st[r], l * 128 + 64 + 16 * ((t - 1) // 2 + 1))
                        apart(pool)
                        pool.dma_start(xt[r], xv[:, t + 1, :]).then_inc(s_xr[r], 16)
                    pool.wait_ge(s_xs, l * 16 + 8 + t + 1)
                    apart(pool)
                    pool.dma_start(xv[:, t, :], xt[t % 2]).then_inc(s_st[t % 2], 16)
                for r in range(2):
                    pool.wait_ge(s_st[r], l * 128 + 128)

        @block.scalar
        def _(act):
            def hi(l, n, np_=P, w=SLOT):
                r = n % 2
                act.wait_ge(s_raw[r], raw_in(l, n))
                act.wait_ge(s_pe, l * SLOTS + n + 1)
                nc.scalar.activation(wsp[0:np_, r, 0, 0:w], raw[0:np_, r, 0:w],
                                     ACT.Copy).then_inc(s_hi, 1)

            def hi_dyn(l, n0, i):
                r = n0 % 2
                act.wait_ge(s_raw[r], l * (8 * SLOTS) + i * 16 + 16 * (L * MODS // 2 + n0 // 2 + 1))
                act.wait_ge(s_pe, l * SLOTS + i * 2 + (n0 + 1))
                nc.scalar.activation(wsp[:, r, 0, :], raw[:, r, :], ACT.Copy).then_inc(s_hi, 1)

            def hi_ff(l, i, q):
                n0 = N_FF + q + 2
                r = n0 % 2
                act.wait_ge(s_raw[r], l * (8 * SLOTS) + i * 32 + 16 * (L * MODS // 2 + n0 // 2 + 1))
                act.wait_ge(s_pe, l * SLOTS + i * 4 + (n0 + 1))
                nc.scalar.activation(wsp[:, r, 0, :], raw[:, r, :], ACT.Copy).then_inc(s_hi, 1)

            def pair(r):
                return ps[:, 2 * r:2 * r + 2, :].rearrange("p a b -> p (a b)")

            act.wait_ge(s_cols, 1)
            nc.scalar.activation(cond[:], W[:, 1024 + 72:1024 + 80], ACT.Silu).then_inc(s_cond, 1)
            act.wait_ge(s_lr, 1)
            nc.scalar.activation(st[:, 4:8], st[:, 0:4], ACT.Exp).then_inc(s_le, 1)
            act.wait_ge(s_par, 1)

            with act.Fori(0, L) as l:
                hi(l, 0, P, KT * LOW)
                hi(l, 1)
                act.wait_ge(s_par, 1)
                for i in range(4):
                    act.wait_ge(s_xl[i], l * 32 + 16)
                    for t in (2 * i, 2 * i + 1):
                        if t:
                            act.wait_ge(s_n1ss, l * 8 + t)
                        nc.scalar.activation(F[:, Fj:Fj + D], F[:, Fx + D * t:Fx + D * t + D],
                                             ACT.Square, accum_out=st[:, S_SS + t:S_SS + t + 1]
                                             ).then_inc(s_n1ss, 1)

                def hT_hi(c0, t):
                    act.wait_ge(s_v, l * 16 + c0 + t + 1)
                    nc.scalar.activation(hT[:, 0, :, t * P:t * P + P],
                                         F[:, Fv4 + D * (t % 4):Fv4 + D * (t % 4) + D]
                                         .rearrange("p (k n) -> p k n", k=KT),
                                         ACT.Copy).then_inc(s_hh, 1)
                for t in range(NT):
                    hT_hi(0, t)

                act.wait_ge(s_pe, l * SLOTS + 1 + CREDIT)
                hi(l, N_WG, LOW, 256)
                nc.scalar.activation(gaT[:, 0, :], pair(0)[0:LOW], ACT.Copy).then_inc(s_gah, 1)
                for n, dst in ((N_GK0, Fgk), (N_WG, None), (N_GK1, Fgk + S), (N_GQ0, Fgq),
                               (N_GQ1, Fgq + S)):
                    act.wait_ge(s_pe, l * SLOTS + n + 1 + CREDIT)
                    hi(l, n + 2)
                    if dst is not None:
                        b = {N_GK0: 1, N_GK1: 0, N_GQ0: 1, N_GQ1: 0}[n]
                        nc.scalar.activation(F[:, dst:dst + S], pair(b), ACT.Copy).then_inc(s_tev, 1)
                act.wait_ge(s_zb, l * 4 + 4)
                nc.scalar.activation(W[:, 0:2048], F[:, Flg:Flg + 2048], ACT.Abs).then_inc(s_ab, 1)
                act.wait_ge(s_ab, l + 1)
                nc.scalar.activation(W[:, 2048:4096], W[:, 0:2048], ACT.Exp, scale=-1.0
                                     ).then_inc(s_ez, 1)
                act.wait_ge(s_ez, l + 1)
                nc.scalar.activation(W[:, 0:2048], W[:, 2048:4096], ACT.Ln, bias=1.0
                                     ).then_inc(s_ln, 1)
                for n in range(N_GV, N_GV + 4):
                    hi(l, n + 2)
                for n in range(N_GR, N_GR + 4):
                    hi(l, n + 2)
                for t in range(NT):
                    if t < NT - 1:
                        act.wait_ge(s_nt, l * 21 + 7 + t + 1)
                    else:
                        act.wait_ge(s_pe, l * SLOTS + N_GR + 4 + CREDIT)
                    nc.scalar.activation(F[:, Fg + 512 * t:Fg + 512 * t + 512], ps[:, t, :],
                                         ACT.Silu).then_inc(s_gr, 1)

                with act.Fori(0, NT // 2) as i:
                    for r in range(2):
                        at = l * NT + i * 2 + r
                        act.wait_ge(s_gD, at + 1)
                        C = tile_of_pairs(Flg, i, r)
                        nc.scalar.activation(We[0].rearrange("p (a n) -> p a n", a=2), C, ACT.Exp,
                                             scale=1.0 / 16.0)
                        nc.scalar.activation(We[1].rearrange("p (a n) -> p a n", a=2), C, ACT.Exp,
                                             scale=-1.0 / 16.0)
                        nc.scalar.activation(We[2], Wd, ACT.Exp, scale=-1.0 / 16.0).then_inc(s_gE, 1)
                        hi_dyn(l, N_DQK + r + 2, i)
                        nc.scalar.activation(F[:, bass.ds(i * (2 * S) + (Fq + r * S), S)], pair(r),
                                             ACT.Copy).then_inc(s_tev, 1)
                        act.wait_ge(s_gC, at + 1)
                        nc.scalar.activation(Wvt, F[:, bass.ds(i * 1024 + (Fv + r * 512), 512)],
                                             ACT.Copy).then_inc(s_gvt, 1)
                        act.wait_ge(s_gO, at + 1)
                        nc.scalar.activation(Wsq, ps[:, 7, :], ACT.Square).then_inc(s_gsq, 1)

                for n in range(N_DV, N_DV + 4):
                    hi(l, n + 2)

                def oT_hi(h, base):
                    act.wait_ge(s_ov, l * 8 + base + 1)
                    nc.scalar.activation(head_of_hT(0, h), Wv, ACT.Copy).then_inc(s_oh, 1)
                for h in range(HEADS):
                    oT_hi(h, h)

                with act.Fori(0, HEADS) as h:
                    u0 = l * 64 + h * 16
                    b0 = l * 32 + h * 8
                    act.wait_ge(s_qk, 1 + u0)
                    act.wait_ge(s_tev, l * 12 + 12)
                    act.wait_ge(s_qz, l + 1)
                    for m in range(2):
                        rows = slice(DK * m, DK * m + DK)
                        last = nc.scalar.activation(Wq[m][rows], F[rows, bass.ds(h * S + Fq, S)],
                                                    ACT.Copy, scale=DK ** -0.5)
                    last.then_inc(s_q, 1)

                    def exps(b, m):
                        n = (b + 1) * P
                        if b >= 2:
                            act.wait_ge(s_at, 1 + b0 + b - 1)
                        else:
                            act.wait_ge(s_at, 1 + b0)
                        act.wait_ge(s_mx, u0 + 2 * b + m + 1)
                        i = 2 * b + m
                        at = Fp + 2048 * (b % 2) + 1024 * m
                        nc.scalar.activation(F[:, at:at + n], pair(m)[:, 0:n], ACT.Exp,
                                             bias=ast[:, A_NM + i:A_NM + i + 1],
                                             accum_out=ast[:, A_R + i:A_R + i + 1]
                                             ).then_inc(s_ex, 1)

                    exps(0, 0)
                    exps(0, 1)
                    for b in range(NT):
                        if b + 1 < NT:
                            exps(b + 1, 0)
                        act.wait_ge(s_at, 1 + b0 + b + 1)
                        act.wait_ge(s_pv, 1 + b0 + b)
                        n = (b + 1) * P
                        nc.scalar.activation(F[:, Fat:Fat + n], pair(2)[:, 0:n], ACT.Copy
                                             ).then_inc(s_ate, 1)
                        if b + 1 < NT:
                            exps(b + 1, 1)
                        act.wait_ge(s_pv, 1 + b0 + b + 1)
                        act.wait_ge(s_asq, 1 + b0 + b)
                        nc.scalar.activation(Wj, ps[:, 6 + b % 2, 0:DV], ACT.Square,
                                             accum_out=ast[:, A_SS + b:A_SS + b + 1]
                                             ).then_inc(s_asq, 1)
                    oT_hi(h + HEADS, h + HEADS)

                def scratch(ys, xs):
                    act.wait_ge(s_ate, 1 + l * 32 + 32)
                    if ys:
                        act.wait_ge(s_yss, l * 16 + ys)
                    if xs:
                        act.wait_ge(s_n2ss, l * 8 + xs)

                def new_y(j, t, junk):
                    if t % 4 < 3:
                        act.wait_ge(s_y, l * 12 + 3 * (j // 4) + t % 4 + 1)
                    else:
                        end = N_OUT + KT * (j // 4 + 1) if j < 8 else N_DOWN + JT * (j // 4 - 1)
                        act.wait_ge(s_pe, l * SLOTS + end + CREDIT)
                    nc.scalar.activation(junk, pair(t % 4), ACT.Square,
                                         accum_out=st[:, S_SS + 8 + t:S_SS + 9 + t]
                                         ).then_inc(s_yss, 1)

                def new_x(t):
                    act.wait_ge(s_xs, l * 16 + t + 1)
                    nc.scalar.activation(F[:, Fj:Fj + D], F[:, Fx + D * t:Fx + D * t + D],
                                         ACT.Square, accum_out=st[:, S_SS + 16 + t:S_SS + 17 + t]
                                         ).then_inc(s_n2ss, 1)

                for g in range(2):
                    for k in range(KT):
                        n = N_OUT + g * KT + k
                        hi(l, n + 2)
                    for i in range(4):
                        t = 4 * g + i
                        scratch(t, t if i == 0 else t - 1)
                        new_y(t, t, F[:, Fj:Fj + D])
                        if i:
                            scratch(t + 1, t - 1)
                            new_x(t - 1)
                    scratch(t + 1, t)
                    new_x(t)
                for t in range(NT):
                    hT_hi(8, t)

                with act.Fori(0, JT // 2) as i:
                    for jj in range(2):
                        act.wait_ge(s_pe, l * SLOTS + i * 4 + (N_FF + 2 * jj + 1 + CREDIT))
                        hi_ff(l, i, 2 * jj)
                        act.wait_ge(s_f2, l * JT + i * 2 + (jj + 1))
                        nc.scalar.activation(W[:, 1024 + 1024 * jj:2048 + 1024 * jj],
                                             pair(2 * jj), ACT.Silu).then_inc(s_f1, 1)
                        hi_ff(l, i, 2 * jj + 1)

                def a_hi(g, k, r, count):
                    act.wait_ge(s_pe, count)
                    nc.scalar.activation(hT[:, 0, r, 0:HALF], F[:, k], ACT.Copy
                                         ).then_inc(s_ah, 1)
                act.wait_ge(s_f2, l * JT + JT + CREDIT)
                for r in range(2):
                    a_hi(0, slice(r * S, r * S + HALF), r, l * SLOTS + N_DOWN + CREDIT)
                for g in range(2):
                    with act.Fori(0, JT // 2 - 1) as i:
                        for r in range(2):
                            n0 = N_DOWN + g * JT + r
                            hi_dyn(l, n0 + 2, i)
                            a_hi(g, bass.ds(i * (2 * S) + ((r + 2) * S + g * HALF), HALF), r,
                                 l * SLOTS + i * 2 + (n0 + 1 + CREDIT))
                    if g == 0:
                        for r in range(2):
                            n = N_DOWN + JT - 2 + r
                            hi(l, n + 2)
                            a_hi(1, slice(r * S + HALF, r * S + S), r,
                                 l * SLOTS + n + 1 + CREDIT)
                    for i in range(4):
                        t = 4 * g + i
                        scratch(8 + t, 8)
                        new_y(8 + t, t, wt[1])

        @block.vector
        def _(dve):
            v = nc.vector

            def pair(r):
                return ps[:, 2 * r:2 * r + 2, :].rearrange("p a b -> p (a b)")

            def lo(l, n, np_=P, w=SLOT):
                r = n % 2
                dve.wait_ge(s_hi, l * SLOTS + n + 1)
                v.tensor_tensor(wsp[0:np_, r, 1, 0:w], raw[0:np_, r, 0:w],
                                wsp[0:np_, r, 0, 0:w].bitcast(F32), ALU.subtract).then_inc(s_lo, 1)

            def lo_dyn(l, n0, i):
                r = n0 % 2
                dve.wait_ge(s_hi, l * SLOTS + i * 2 + (n0 + 1))
                v.tensor_tensor(wsp[:, r, 1, :], raw[:, r, :], wsp[:, r, 0, :].bitcast(F32),
                                ALU.subtract).then_inc(s_lo, 1)

            def lo_ff(l, i, q):
                n0 = N_FF + q + 2
                r = n0 % 2
                dve.wait_ge(s_hi, l * SLOTS + i * 4 + (n0 + 1))
                v.tensor_tensor(wsp[:, r, 1, :], raw[:, r, :], wsp[:, r, 0, :].bitcast(F32),
                                ALU.subtract).then_inc(s_lo, 1)

            dve.sem_inc(s_lo, CREDIT)
            dve.sem_inc(s_pe, CREDIT)
            dve.sem_inc(s_mod, CREDIT)
            dve.sem_inc(s_f2, CREDIT)
            for s in (s_al, s_yu, s_gG, s_ex, s_ate,
                      s_on, s_qk, s_at, s_pv, s_gE, s_asq, s_ol):
                dve.sem_inc(s, 1)
            v.memset(ones[:], 1.0).then_inc(s_ones, 1)
            dve.wait_ge(s_ones, 1)

            dve.wait_ge(s_small, 16 * 9)
            v.memset(F[BUCKETS:BUCKETS + 1, 768:768 + HEADS], MASKED).then_inc(s_rx, 1)
            dve.wait_ge(s_rx, 1)
            v.tensor_copy(F[0:BUCKETS + 1, 1536:2048].rearrange("p (h n) -> p h n", h=HEADS),
                          F[0:BUCKETS + 1, 768:768 + HEADS].unsqueeze(2)
                          .to_broadcast([BUCKETS + 1, HEADS, P])).then_inc(s_rx, 1)
            dve.wait_ge(s_rows, 1)
            cols = W[:, 1024:1024 + 2 * P]
            v.tensor_copy(cols[:, 0:80], ps[:, 1, 0:80])
            v.tensor_copy(cols[:, P:P + L * MODS], ps[:, 1, P:P + L * MODS]).then_inc(s_cols, 1)
            dve.wait_ge(s_cols, 1)
            for h in range(HEADS):
                dve.wait_ge(s_rb, h + 1)
                v.tensor_copy(F[:, 2048 + 384 * h:2432 + 384 * h], ps[:, 2 + h, 0:384]
                              ).then_inc(s_rbs, 1)
            lw = F[:, 256:768].rearrange("p (a i d) -> p a i d", i=2, d=DK)
            v.tensor_tensor(W[:, 2048:2304].rearrange("p (a d) -> p a d", a=4), lw[:, :, 0],
                            lw[:, :, 1], ALU.mult).then_inc(s_lp, 1)
            dve.wait_ge(s_lp, 1)
            v.tensor_reduce(st[:, 0:4], W[:, 2048:2304].rearrange("p (a d) -> p a d", a=4),
                            AX.X, ALU.add).then_inc(s_lr, 1)
            dve.wait_ge(s_le, 1)
            for l in range(L):
                v.scalar_tensor_tensor(par[:, l, P_LAM:P_LAM + 1], st[:, 4 + 2 * l + 1:4 + 2 * l + 2],
                                       cst[:, C_LAM + 2 * l:C_LAM + 2 * l + 1],
                                       st[:, 4 + 2 * l:4 + 2 * l + 1], ALU.subtract, ALU.subtract)
                v.tensor_copy(par[:, l, P_GN:P_GN + 1], cols[:, 64 + l:65 + l])
                v.tensor_scalar(par[:, l, P_DN:P_DN + 1], cols[:, 66 + l:67 + l],
                                cst[:, C_LAM + 2 * l + 1:C_LAM + 2 * l + 2], None, ALU.mult)
                v.tensor_copy(par[:, l, P_BG:P_BG + 2], cols[:, 68 + 2 * l:70 + 2 * l])
            dve.wait_ge(s_mod, L * MODS + CREDIT)
            mod = W[:, 2304:2304 + L * MODS]
            v.tensor_tensor(mod, ps[:, 0, 0:L * MODS], cols[:, P:P + L * MODS], ALU.add
                            ).then_inc(s_modv, 1)
            dve.wait_ge(s_modv, 1)
            for l in range(L):
                for s in range(2):
                    m = [mod[:, l * MODS + (3 * s + i) * KT:l * MODS + (3 * s + i + 1) * KT]
                         for i in range(3)]
                    gn = [cols[:, l * 32 + (2 * s + i) * KT:l * 32 + (2 * s + i + 1) * KT]
                          for i in range(2)]
                    q = [par[:, l, 24 * s + a:24 * s + a + KT] for a in (P_A, P_B, P_G)]
                    v.scalar_tensor_tensor(q[0], m[1], 1.0, gn[0], ALU.add, ALU.mult)
                    v.tensor_copy(q[1], m[0])
                    last = v.tensor_tensor(q[2], m[2], gn[1], ALU.mult)
            last.then_inc(s_par, 1)
            dve.wait_ge(s_par, 1)

            with dve.Fori(0, L) as l:
                v.tensor_copy(cur[:], par[:, l, :]).then_inc(s_cur, 1)
                lo(l, 0, P, KT * LOW)
                lo(l, 1)
                dve.wait_ge(s_n1ss, l * 8 + 8)
                v.tensor_scalar(st[:, S_MS:S_MS + 8], st[:, S_SS:S_SS + 8], 1.0 / D, EPS,
                                ALU.mult, ALU.add).then_inc(s_n1ms, 1)
                dve.wait_ge(s_n1rs, l + 1)
                for t in range(NT):
                    v.tensor_scalar(F[:, Fxn + D * t:Fxn + D * t + D], F[:, Fx + D * t:Fx + D * t + D],
                                    st[:, S_RS + t:S_RS + t + 1], None, ALU.mult).then_inc(s_xn, 1)
                dve.wait_ge(s_cur, l + 1)

                def hT_v(c0, t):
                    dve.wait_ge(s_tr, l * 16 + c0 + t + 1)
                    a = P_A + (24 if c0 else 0)
                    for k in range(KT):
                        o = Fv4 + D * (t % 4) + P * k
                        last = v.tensor_scalar(F[:, o:o + P], pair(t % 4)[:, P * k:P * k + P],
                                               cur[:, a + k:a + k + 1], cur[:, a + KT + k:a + KT + k + 1],
                                               ALU.mult, ALU.add)
                    last.then_inc(s_v, 1)

                def hT_lo(c0, t):
                    dve.wait_ge(s_hh, l * 16 + c0 + t + 1)
                    v.tensor_tensor(hT[:, 1, :, t * P:t * P + P],
                                    kn(F[:, Fv4 + D * (t % 4):Fv4 + D * (t % 4) + D]),
                                    hT[:, 0, :, t * P:t * P + P].bitcast(F32),
                                    ALU.subtract).then_inc(s_hl, 1)

                def norm_out(c0):
                    for t in range(NT + 1):
                        if t < NT:
                            hT_v(c0, t)
                        if t:
                            hT_lo(c0, t - 1)
                norm_out(0)

                lo(l, N_WG, LOW, 256)
                dve.wait_ge(s_gah, l + 1)
                v.tensor_tensor(gaT[:, 1, :], pair(0)[0:LOW], gaT[:, 0, :].bitcast(F32),
                                ALU.subtract).then_inc(s_gal, 1)
                lo(l, N_GK0 + 2)
                lo(l, N_WG + 2)
                for i in range(4):
                    o = Flg + 512 * i
                    v.tensor_scalar(F[:, o:o + 512], ps[:, 4 + i, :],
                                    cur[:, P_BG + i // 2:P_BG + i // 2 + 1], None,
                                    ALU.add).then_inc(s_zb, 1)
                lo(l, N_GK1 + 2)
                lo(l, N_GQ0 + 2)
                lo(l, N_GQ1 + 2)
                dve.wait_ge(s_ln, l + 1)
                v.scalar_tensor_tensor(F[:, Flg:Flg + 2048], F[:, Flg:Flg + 2048], 0.0,
                                       W[:, 0:2048], ALU.min, ALU.subtract).then_inc(s_lg, 1)
                for n in range(N_GV, N_GV + 4):
                    lo(l, n + 2)
                for t in range(NT):
                    if t < NT - 1:
                        dve.wait_ge(s_nt, l * 21 + t + 1)
                    else:
                        dve.wait_ge(s_pe, l * SLOTS + N_GV + 4 + CREDIT)
                    v.tensor_copy(F[:, Fv + 512 * t:Fv + 512 * t + 512], ps[:, t, :]
                                  ).then_inc(s_gv, 1)
                for n in range(N_GR, N_GR + 4):
                    lo(l, n + 2)

                dve.wait_ge(s_lg, l + 1)
                v.memset(W[:, 1024:2048], 0.0).then_inc(s_gz, 1)
                v.memset(Ws[0], 0.0).then_inc(s_gs0, 1)
                dve.wait_ge(s_gz, l + 1)
                apart(dve)
                with dve.Fori(0, NT // 2) as i:
                    for r in range(2):
                        at = l * NT + i * 2 + r
                        C = tile_of_pairs(Flg, i, r)
                        for p in range(2):
                            for e in range(2):
                                cc = F[:, bass.ds(i * (2 * P) + (Flg + p * S + r * P + e * CH), CH)]
                                last = v.tensor_tensor_scan(cc, ones[:, 0:CH], cc, 0.0,
                                                            ALU.mult, ALU.add)
                        last.then_inc(s_gsc, 1)
                        dve.wait_ge(s_gsc, at + 1)
                        dve.wait_ge(s_gE, 1 + at)
                        for p in range(2):
                            Cp = F[:, bass.ds(i * (2 * P) + (Flg + p * S + r * P), P)].rearrange(
                                "p (e n) -> p e n", e=2)
                            last = v.tensor_tensor(
                                Wd[:, p * P:p * P + P].rearrange("p (e n) -> p e n", e=2), Cp,
                                Cp[:, :, CH - 1:CH].to_broadcast([P, 2, CH]), ALU.subtract)
                        last.then_inc(s_gD, 1)
                        dve.wait_ge(s_gE, 1 + at + 1)
                        if True:
                            q = tile_of_pairs(Fgq, i, r)
                            k = tile_of_pairs(Fgk, i, r)
                            a2 = lambda z: z.rearrange("p (a n) -> p a n", a=2)
                            for z in range(2):
                                own = slice(DK * z, DK * z + DK)
                                v.scalar_tensor_tensor(a2(Wqe[r][z])[own], q[own], DK ** -0.5,
                                                       a2(We[0])[own], ALU.mult, ALU.mult)
                            v.tensor_tensor(a2(Wke[r]), k, a2(We[1]), ALU.mult)
                            v.tensor_tensor(a2(Wkd[r]), k, a2(We[2]), ALU.mult).then_inc(s_gC, 1)
                        dve.wait_ge(s_gA, at + 1)
                        v.tensor_copy(Wkn[r], ps[:, 4, 0:256])
                        v.tensor_tensor(Wam.rearrange("p (h n) -> p h n", h=HEADS),
                                        ps[:, 5, :].rearrange("p (h n) -> p h n", h=HEADS),
                                        gmask.unsqueeze(1).to_broadcast([P, HEADS, P]),
                                        ALU.mult).then_inc(s_gd, 1)
                        lo_dyn(l, N_DQK + r + 2, i)
                        dve.wait_ge(s_gU, at + 1)
                        for e in range(2):
                            if e == 0 and r == 0:
                                dve.wait_ge(s_gs0, l + 1)
                            for p in range(2):
                                src, dst = Ws[2 * r + e], Ws[(2 * r + e + 1) % 4]
                                d = We[0][:, p * P + e * CH + CH - 1:p * P + e * CH + CH]
                                last = v.scalar_tensor_tensor(
                                    dst[:, p * P:p * P + P], src[:, p * P:p * P + P], d,
                                    ps[:, 6 - 2 * e, p * P:p * P + P], ALU.mult, ALU.add)
                            last.then_inc(s_gS, 1)
                            dve.wait_ge(s_gS, at * 2 + (e + 1))
                        dve.wait_ge(s_gsq, at + 1)
                        v.tensor_reduce(st[:, S_GSS:S_GSS + 4], Wsq.rearrange("p (h n) -> p h n", h=4),
                                        AX.X, ALU.add).then_inc(s_gss, 1)
                        dve.wait_ge(s_gss, at + 1)
                        v.tensor_scalar(st[:, S_GMS:S_GMS + 4], st[:, S_GSS:S_GSS + 4], 1.0 / DV, EPS,
                                        ALU.mult, ALU.add).then_inc(s_gms, 1)
                        dve.wait_ge(s_grs, at + 1)
                        for h in range(HEADS):
                            o = F[:, bass.ds(i * 1024 + (Fg + r * 512 + h * DV), DV)]
                            last = v.scalar_tensor_tensor(
                                o, ps[:, 7, h * DV:(h + 1) * DV], st[:, S_GRS + h:S_GRS + h + 1], o,
                                ALU.mult, ALU.mult)
                        last.then_inc(s_gG, 1)

                for n in range(N_DV, N_DV + 4):
                    lo(l, n + 2)
                for t in range(NT):
                    if t < NT - 1:
                        dve.wait_ge(s_nt, l * 21 + 14 + t + 1)
                    else:
                        dve.wait_ge(s_pe, l * SLOTS + N_DV + 4 + CREDIT)
                    v.tensor_copy(F[:, Fv + 512 * t:Fv + 512 * t + 512], ps[:, t, :]
                                  ).then_inc(s_dv, 1)

                def oT_vl(h, j, gain):
                    dve.wait_ge(s_oT, l * 8 + j + 1)
                    dve.wait_ge(s_ol, 1 + l * 8 + j)
                    v.tensor_scalar(Wv, pair(2), cur[:, gain:gain + 1], None, ALU.mult
                                    ).then_inc(s_ov, 1)
                    dve.wait_ge(s_oh, l * 8 + j + 1)
                    v.tensor_tensor(head_of_hT(1, h), Wv, head_of_hT(0, h).bitcast(F32),
                                    ALU.subtract).then_inc(s_ol, 1)
                for h in range(HEADS):
                    oT_vl(h, h, P_GN)

                v.memset(Wq[0][DK:P], 0.0)
                v.memset(Wq[1][0:DK], 0.0).then_inc(s_qz, 1)
                dve.wait_ge(s_bias, l * 16 + 16)
                apart(dve)
                with dve.Fori(0, HEADS) as h:
                    u0 = l * 64 + h * 16
                    b0 = l * 32 + h * 8

                    def maxes(b, m):
                        n, i = (b + 1) * P, 2 * b + m
                        w = min(n, NEAR)
                        dve.wait_ge(s_qk, 1 + u0 + i + 1)
                        near = pair(m)[:, n - w:n]
                        v.tensor_tensor(near, near, F[:, bass.ds(h * NEAR + (Fbias + NEAR - w), w)],
                                        ALU.add).then_inc(s_ba, 1)
                        dve.wait_ge(s_ba, u0 + i + 1)
                        v.reduce_max(ast[:, A_MX + i:A_MX + i + 1], pair(m)[:, 0:n], AX.X
                                     ).then_inc(s_mr, 1)
                        dve.wait_ge(s_mr, u0 + i + 1)
                        v.tensor_scalar(ast[:, A_NM + i:A_NM + i + 1], ast[:, A_MX + i:A_MX + i + 1],
                                        -1.0, None, ALU.mult).then_inc(s_mx, 1)

                    def combine(b):
                        n, i = (b + 1) * P, 2 * b
                        dve.wait_ge(s_ex, 1 + u0 + i + 2)
                        v.reciprocal(ast[:, A_RI + i:A_RI + i + 2], ast[:, A_R + i:A_R + i + 2]
                                     ).then_inc(s_rc, 1)
                        dve.wait_ge(s_rc, b0 + b + 1)
                        v.tensor_scalar(ast[:, A_CO + b:A_CO + b + 1], ast[:, A_R + i:A_R + i + 1],
                                        ast[:, A_RI + i + 1:A_RI + i + 2], cur[:, P_LAM:P_LAM + 1],
                                        ALU.mult, ALU.mult).then_inc(s_co, 1)
                        dve.wait_ge(s_co, b0 + b + 1)
                        p0 = F[:, Fp + 2048 * (b % 2):Fp + 2048 * (b % 2) + n]
                        p1 = F[:, Fp + 2048 * (b % 2) + 1024:Fp + 2048 * (b % 2) + 1024 + n]
                        v.scalar_tensor_tensor(p0, p1, ast[:, A_CO + b:A_CO + b + 1], p0,
                                               ALU.mult, ALU.add).then_inc(s_ad, 1)

                    def mean(b):
                        dve.wait_ge(s_asq, 1 + b0 + b + 1)
                        ri = ast[:, A_RI + 2 * b:A_RI + 2 * b + 1]
                        v.tensor_scalar(ast[:, A_M1 + b:A_M1 + b + 1], ast[:, A_SS + b:A_SS + b + 1],
                                        ri, ri, ALU.mult, ALU.mult).then_inc(s_am1, 1)
                        dve.wait_ge(s_am1, b0 + b + 1)
                        v.tensor_scalar(ast[:, A_MS + b:A_MS + b + 1], ast[:, A_M1 + b:A_M1 + b + 1],
                                        1.0 / DV, EPS, ALU.mult, ALU.add).then_inc(s_ams, 1)

                    def normed(b):
                        dve.wait_ge(s_ars, b0 + b + 1)
                        if b == 0:
                            dve.wait_ge(s_oT, l * 8 + h + 4)
                        v.tensor_scalar(Won[:, b * DV:(b + 1) * DV], ps[:, 6 + b % 2, 0:DV],
                                        ast[:, A_RS + b:A_RS + b + 1],
                                        ast[:, A_RI + 2 * b:A_RI + 2 * b + 1],
                                        ALU.mult, ALU.mult).then_inc(s_on, 1)

                    maxes(0, 0)
                    maxes(0, 1)
                    for b in range(NT):
                        if b + 1 < NT:
                            maxes(b + 1, 0)
                        combine(b)
                        if b >= 2:
                            normed(b - 2)
                        if b + 1 < NT:
                            maxes(b + 1, 1)
                        if b >= 1:
                            mean(b - 1)
                    normed(NT - 2)
                    mean(NT - 1)
                    normed(NT - 1)
                    oT_vl(h + HEADS, h + HEADS, P_DN)

                def gate_row(s):
                    for k in range(KT):
                        a = P_G + 24 * s + k
                        last = v.tensor_scalar(diag[:, k, :], ident, cur[:, a:a + 1], None, ALU.mult)
                    last.then_inc(s_dg, 1)
                    dve.wait_ge(s_gbp, l * 2 + s + 1)
                    v.tensor_copy(gb, pair(0)).then_inc(s_gb, 1)

                def y_mean(j, t):
                    dve.wait_ge(s_yss, l * 16 + j + 1)
                    v.tensor_scalar(st[:, S_MS + 8 + t:S_MS + 9 + t], st[:, S_SS + 8 + t:S_SS + 9 + t],
                                    1.0 / D, EPS, ALU.mult, ALU.add).then_inc(s_yms, 1)

                def y_add(j, t, tmp, xtile):
                    dve.wait_ge(s_yrs, l * 16 + j + 1)
                    if j >= 1:
                        dve.wait_ge(s_xs, l * 16 + j)
                    v.scalar_tensor_tensor(tmp, pair(t % 4), st[:, S_RS + 8 + t:S_RS + 9 + t], gb,
                                           ALU.mult, ALU.mult).then_inc(s_yu, 1)
                    dve.wait_ge(s_yu, 1 + l * 16 + j + 1)
                    v.tensor_tensor(xtile, xtile, tmp, ALU.add).then_inc(s_xs, 1)

                def x_norm(t):
                    dve.wait_ge(s_n2ss, l * 8 + t + 1)
                    v.tensor_scalar(st[:, S_MS + 16 + t:S_MS + 17 + t],
                                    st[:, S_SS + 16 + t:S_SS + 17 + t],
                                    1.0 / D, EPS, ALU.mult, ALU.add).then_inc(s_n2ms, 1)
                    dve.wait_ge(s_n2rs, l * 8 + t + 1)
                    v.tensor_scalar(F[:, Fxn + D * t:Fxn + D * t + D], F[:, Fx + D * t:Fx + D * t + D],
                                    st[:, S_RS + 16 + t:S_RS + 17 + t], None, ALU.mult
                                    ).then_inc(s_xn, 1)

                gate_row(0)
                dve.wait_ge(s_gb, l * 2 + 1)
                for g in range(2):
                    for k in range(KT):
                        lo(l, N_OUT + g * KT + k + 2)
                    y_mean(4 * g, 4 * g)
                    for i in range(4):
                        t = 4 * g + i
                        if i < 3:
                            y_mean(t + 1, t + 1)
                        dve.wait_ge(s_xl[t // 2], l * 32 + 32)
                        y_add(t, t, wt[t % 2], F[:, Fx + D * t:Fx + D * t + D])
                        if i:
                            x_norm(t - 1)
                    x_norm(4 * g + 3)
                norm_out(8)

                for r in range(2):
                    dve.wait_ge(s_st[r], l * 128 + 64)
                apart(dve)
                with dve.Fori(0, JT // 2) as i:
                    for jj in range(2):
                        lo_ff(l, i, 2 * jj)
                        lo_ff(l, i, 2 * jj + 1)
                        dve.wait_ge(s_f1, l * JT + i * 2 + (jj + 1))
                        dve.wait_ge(s_pe, l * SLOTS + i * 4 + (N_FF + 2 * jj + 2 + CREDIT))
                        v.tensor_tensor(F[:, bass.ds(i * 2048 + jj * 1024, 1024)],
                                        W[:, 1024 + 1024 * jj:2048 + 1024 * jj], pair(2 * jj + 1),
                                        ALU.mult).then_inc(s_f2, 1)
                gate_row(1)
                dve.wait_ge(s_gb, l * 2 + 2)

                def a_lo(src, r, count):
                    dve.wait_ge(s_ah, count)
                    v.tensor_tensor(hT[:, 1, r, 0:HALF], F[:, src], hT[:, 0, r, 0:HALF].bitcast(F32),
                                    ALU.subtract).then_inc(s_al, 1)
                for r in range(2):
                    a_lo(slice(r * S, r * S + HALF), r, l * (2 * JT) + r + 1)
                for g in range(2):
                    with dve.Fori(0, JT // 2 - 1) as i:
                        for r in range(2):
                            lo_dyn(l, N_DOWN + g * JT + r + 2, i)
                            a_lo(bass.ds(i * (2 * S) + ((r + 2) * S + g * HALF), HALF), r,
                                 l * (2 * JT) + i * 2 + (g * JT + r + 3))
                    if g == 0:
                        for r in range(2):
                            lo(l, N_DOWN + JT + r)
                            a_lo(slice(r * S + HALF, r * S + S), r, l * (2 * JT) + JT + r + 1)
                    y_mean(8 + 4 * g, 4 * g)
                    for i in range(4):
                        t = 4 * g + i
                        if i < 3:
                            y_mean(8 + t + 1, t + 1)
                        dve.wait_ge(s_xr[t % 2], l * 64 + 16 * (t // 2 + 1))
                        y_add(8 + t, t, wt[0], xt[t % 2])

        @block.tensor
        def _(pe):
            mm = nc.tensor.matmul

            def pair(r):
                return ps[:, 2 * r:2 * r + 2, :].rearrange("p a b -> p (a b)")

            def three(o, a, b, start, stop):
                mm(o, a(0), b(0), start=start, stop=False)
                mm(o, a(0), b(1), start=False, stop=False)
                return mm(o, a(1), b(0), start=False, stop=stop)

            pe.wait_ge(s_cst, 16)
            pe.wait_ge(s_small, 16 * 9)
            nc.tensor.transpose(ps[:, 1, 0:80], F[0:80, 0:P], ident[0:80, 0:80])
            nc.tensor.transpose(ps[:, 1, P:P + L * MODS], F[0:L * MODS, P:2 * P],
                                ident[0:L * MODS, 0:L * MODS]).then_inc(s_rows, 1)
            pe.wait_ge(s_rx, 2)
            for h in range(HEADS):
                mm(ps[:, 2 + h, 0:3 * P], F[0:BUCKETS + 1, 1536 + P * h:1536 + P * h + P],
                   F[0:BUCKETS + 1, 1024:1024 + 3 * P], start=True, stop=True).then_inc(s_rb, 1)
            pe.wait_ge(s_cond, 1)
            with pe.Fori(0, L * MODS // 2) as j:
                for r in range(2):
                    pe.wait_ge(s_raw[r], j * 16 + 16)
                    o = ps[:, 0, bass.ds(j * 2 + r, 1)]
                    for k in range(KT):
                        last = mm(o, raw[:, r, k * P:k * P + P], cond[:, k:k + 1],
                                  start=(k == 0), stop=(k == KT - 1))
                    last.then_inc(s_mod, 1)
            pe.wait_ge(s_ones, 1)
            pe.wait_ge(s_modv, 1)

            with pe.Fori(0, L) as l:
                def split(n):
                    pe.wait_ge(s_lo, l * SLOTS + n + 1 + CREDIT)

                def norm_tr(c0, t):
                    pe.wait_ge(s_xn, l * 16 + c0 + t + 1)
                    if t >= 4:
                        pe.wait_ge(s_v, l * 16 + c0 + t - 3)
                    elif c0:
                        pe.wait_ge(s_yu, 1 + l * 16 + 4 + t + 1)
                    else:
                        pe.wait_ge(s_yu, 1 + l * 16)
                    for k in range(KT):
                        o = Fxn + D * t + P * k
                        last = nc.tensor.transpose(pair(t % 4)[:, P * k:P * k + P], F[:, o:o + P], ident)
                    last.then_inc(s_tr, 1)

                for t in range(NT):
                    norm_tr(0, t)

                def columns(n_parity, b, halves=(0, 1), w=P, m=P):
                    r = n_parity
                    for hf in halves:
                        for k in range(KT):
                            last = three(pair(b)[0:m, HALF * hf:HALF * hf + HALF],
                                         lambda z: wsp[:, r, z, k * w:k * w + w],
                                         lambda z: hT[:, z, k, HALF * hf:HALF * hf + HALF],
                                         k == 0, k == KT - 1)
                    return last

                pe.wait_ge(s_hl, l * 16 + 8)
                split(N_GA)
                columns(0, 0, w=LOW, m=LOW).then_inc(s_pe, 1)
                split(N_GK0)
                columns(1, 1).then_inc(s_pe, 1)
                split(N_WG)
                pe.wait_ge(s_gal, l + 1)
                for i in range(4):
                    p, hf = i // 2, i % 2
                    last = three(ps[:, 4 + i, :], lambda z: wsp[0:LOW, 0, z, p * P:p * P + P],
                                 lambda z: gaT[:, z, hf * HALF:hf * HALF + HALF], True, True)
                last.then_inc(s_pe, 1)
                split(N_GK1)
                columns(1, 0).then_inc(s_pe, 1)
                split(N_GQ0)
                pe.wait_ge(s_tev, l * 12 + 1)
                columns(0, 1).then_inc(s_pe, 1)
                split(N_GQ1)
                pe.wait_ge(s_tev, l * 12 + 2)
                columns(1, 0).then_inc(s_pe, 1)

                def rows(n0, free):
                    for i in range(4):
                        n = n0 + i
                        split(n)
                        for t in range(NT):
                            if i == 0:
                                free(t)
                            for kk in range(2):
                                k = 2 * i + kk
                                last = three(ps[:, t, :], lambda z: hT[:, z, k, t * P:t * P + P],
                                             lambda z: wsp[:, n % 2, z, kk * 512:kk * 512 + 512],
                                             k == 0, k == KT - 1)
                            if i == 3 and t < NT - 1:
                                last.then_inc(s_nt, 1)
                        last.then_inc(s_pe, 1)

                def free_gv(t):
                    pe.wait_ge(s_tev, l * 12 + 4)
                    pe.wait_ge(s_zb, l * 4 + 4)
                rows(N_GV, free_gv)
                rows(N_GR, lambda t: pe.wait_ge(s_gv, l * 8 + t + 1))

                pe.wait_ge(s_gr, l * 8 + 8)
                apart(pe)
                with pe.Fori(0, NT // 2) as i:
                    for r in range(2):
                        at = l * NT + i * 2 + r
                        n = N_DQK + r
                        pe.wait_ge(s_lo, l * SLOTS + i * 2 + (n + 1 + CREDIT))
                        pe.wait_ge(s_tev, l * 12 + i * 2 + (4 + r - 1))
                        columns(r, r, (0,))
                        pe.wait_ge(s_gC, at + 1)
                        pe.wait_ge(s_gG, 1 + at)
                        for p in range(2):
                            nc.tensor.transpose(ps[:, 4, p * P:p * P + P], Wkd[r][:, p * P:p * P + P],
                                                ident)
                        for h in range(HEADS):
                            p, b = h // 2, DK * (h % 2)
                            last = mm(ps[:, 5, h * P:h * P + P], Wke[r][:, p * P:p * P + P],
                                      Wqe[r][h % 2][:, p * P:p * P + P], start=True, stop=True)
                        last.then_inc(s_gA, 1)
                        columns(r, r, (1,)).then_inc(s_pe, 1)
                        pe.wait_ge(s_gd, at + 1)
                        pe.wait_ge(s_gvt, at + 1)
                        apart(pe)
                        for e in range(2):
                            for h in range(HEADS):
                                p, b = h // 2, DK * (h % 2)
                                vv = Wvt[e * CH:e * CH + CH, h * DV:h * DV + DV]
                                last = mm(ps[b:b + DK, 6 - 2 * e, p * P:p * P + P],
                                          Wkn[r][e * CH:e * CH + CH, p * P + b:p * P + b + DK], vv,
                                          start=True, stop=True)
                        last.then_inc(s_gU, 1)
                        pe.wait_ge(s_gS, at * 2 + 1)
                        for h in range(HEADS):
                            p, b = h // 2, DK * (h % 2)
                            o = ps[:, 7, h * DV:(h + 1) * DV]
                            mm(o, Wam[:, h * P:h * P + P], Wvt[:, h * DV:h * DV + DV],
                               start=True, stop=False, skip_group_check=True)
                            for e in range(2):
                                last = mm(o[e * CH:e * CH + CH],
                                          Wqe[r][h % 2][:, p * P + e * CH:p * P + e * CH + CH],
                                          Ws[2 * r + e][:, p * P:p * P + P],
                                          start=False, stop=(e == 1), skip_group_check=True)
                        last.then_inc(s_gO, 1)

                pe.wait_ge(s_gG, 1 + l * NT + NT)
                pe.wait_ge(s_tev, l * 12 + 12)
                rows(N_DV, lambda t: None)

                def to_features(j, src):
                    for t in range(NT):
                        last = nc.tensor.transpose(pair(2)[:, t * P:t * P + P], src(t), ident)
                    last.then_inc(s_oT, 1)
                for h in range(HEADS):
                    if h == 0:
                        pe.wait_ge(s_dv, l * 8 + 8)
                    else:
                        pe.wait_ge(s_ov, l * 8 + h)
                    to_features(h, lambda t: F[:, Fg + 512 * t + DV * h:Fg + 512 * t + DV * h + DV])
                pe.wait_ge(s_ov, l * 8 + 4)
                apart(pe)

                with pe.Fori(0, HEADS) as h:
                    u0 = l * 64 + h * 16
                    b0 = l * 32 + h * 8

                    def scores(b, m):
                        n = (b + 1) * P
                        if b:
                            pe.wait_ge(s_ex, 1 + u0 + 2 * b + m - 1)
                        else:
                            pe.wait_ge(s_ex, 1 + u0)
                        for c0 in range(0, n, 512):
                            w = min(512, n - c0)
                            last = mm(pair(m)[:, c0:c0 + w],
                                      Wq[m][:, b * P:b * P + P],
                                      F[:, bass.ds(h * S + (Fk + c0), w)],
                                      start=True, stop=True)
                        last.then_inc(s_qk, 1)

                    pe.wait_ge(s_q, l * HEADS + h + 1)
                    pe.wait_ge(s_ov, l * 8 + h + 4)
                    scores(0, 0)
                    scores(0, 1)
                    for b in range(NT):
                        if b + 1 < NT:
                            scores(b + 1, 0)
                        pe.wait_ge(s_ad, b0 + b + 1)
                        pe.wait_ge(s_ate, 1 + b0 + b)
                        for t in range(b + 1):
                            o = Fp + 2048 * (b % 2) + P * t
                            last = nc.tensor.transpose(pair(2)[:, t * P:t * P + P], F[:, o:o + P], ident)
                        last.then_inc(s_at, 1)
                        if b + 1 < NT:
                            scores(b + 1, 1)
                        pe.wait_ge(s_ate, 1 + b0 + b + 1)
                        if b >= 2:
                            pe.wait_ge(s_on, 1 + b0 + b - 1)
                        else:
                            pe.wait_ge(s_on, 1 + b0)
                        for t in range(b + 1):
                            last = mm(ps[:, 6 + b % 2, 0:DV], F[:, Fat + P * t:Fat + P * t + P],
                                      F[:, bass.ds(h * DV + (Fv + 512 * t), DV)],
                                      start=(t == 0), stop=(t == b))
                        last.then_inc(s_pv, 1)
                    pe.wait_ge(s_on, 1 + b0 + 8)
                    to_features(h + HEADS, lambda t: Won[:, t * DV:t * DV + DV])

                def gate_row(s):
                    pe.wait_ge(s_dg, l * 2 + s + 1)
                    for k in range(KT):
                        last = mm(pair(0)[:, k * P:k * P + P], ones[:], diag[:, k, :],
                                  start=True, stop=True)
                    last.then_inc(s_gbp, 1)
                    pe.wait_ge(s_gb, l * 2 + s + 1)

                def down(hs, r, first, last_k, j0, free):
                    for i in range(4):
                        if first:
                            free(i)
                        for z, zz in ((0, 0), (0, 1), (1, 0)):
                            for c in range(2):
                                last = mm(pair(i)[:, 512 * c:512 * c + 512], hs(z, i),
                                          wsp[:, r, zz, 512 * c:512 * c + 512],
                                          start=first and z == 0 and zz == 0,
                                          stop=last_k and z == 1)
                        if last_k and i < 3:
                            last.then_inc(s_y, 1)
                    last.then_inc(s_pe, 1)

                gate_row(0)
                pe.wait_ge(s_ol, 1 + l * 8 + 8)
                for g in range(2):
                    def free(i):
                        if g:
                            pe.wait_ge(s_yu, 1 + l * 16 + i + 1)
                    for k in range(KT):
                        n = N_OUT + g * KT + k
                        split(n)
                        down(lambda z, i: hT[:, z, k, (4 * g + i) * P:(4 * g + i + 1) * P], n % 2,
                             k == 0, k == KT - 1, 0, free)
                for t in range(NT):
                    norm_tr(8, t)

                pe.wait_ge(s_hl, l * 16 + 16)
                apart(pe)
                with pe.Fori(0, JT // 2) as i:
                    for jj in range(2):
                        pe.wait_ge(s_f2, l * JT + i * 2 + (jj + 1))
                        for r in range(2):
                            pe.wait_ge(s_lo, l * SLOTS + i * 4 + (N_FF + 2 * jj + r + 1 + CREDIT))
                            columns(r, 2 * jj + r).then_inc(s_pe, 1)
                pe.wait_ge(s_f2, l * JT + JT + CREDIT)
                gate_row(1)
                for g in range(2):
                    def free(i):
                        if g:
                            pe.wait_ge(s_yu, 1 + l * 16 + 8 + i + 1)

                    def acts(r):
                        return lambda z, i: hT[:, z, r, i * P:i * P + P]
                    for r in range(2):
                        n = N_DOWN + g * JT + r
                        split(n)
                        pe.wait_ge(s_al, 1 + l * (2 * JT) + g * JT + r + 1)
                        down(acts(r), r, r == 0, False, 0, free)
                    with pe.Fori(1, JT // 2 - 1) as i:
                        for r in range(2):
                            pe.wait_ge(s_lo, l * SLOTS + i * 2 + (N_DOWN + g * JT + r + 1 + CREDIT))
                            pe.wait_ge(s_al, 1 + l * (2 * JT) + i * 2 + (g * JT + r + 1))
                            down(acts(r), r, False, False, 0, free)
                    for r in range(2):
                        n = N_DOWN + g * JT + JT - 2 + r
                        split(n)
                        pe.wait_ge(s_al, 1 + l * (2 * JT) + g * JT + JT - 2 + r + 1)
                        down(acts(r), r, False, r == 1, 0, free)


_INS = ["x", "c", "w_mod", "b_mod", "norm_gains", "w_in", "w_gla_gate", "b_gla_gate", "gla_norm",
        "diff_lambda", "diff_norm", "rel_bias", "w_out", "w_gate_up", "w_down"]


def kernel(**inputs):
    import concourse.bacc as bacc
    from concourse.bass_utils import run_bass_kernel_spmd

    nc = bacc.Bacc("TRN2", target_bir_lowering=False, num_devices=1)
    arrays, args = {}, []
    consts, hot = layer_constants()
    given = [(k, np.ascontiguousarray(inputs[k])) for k in _INS] + [("consts", consts), ("onehot", hot)]
    for name, a in given:
        if name == "x":
            a = a.reshape(S, D)
        arrays[f"in_{name}"] = a
        args.append(nc.dram_tensor(f"in_{name}", a.shape, F32, kind="ExternalInput").ap())
    args.append(nc.dram_tensor("bias_rows", (HEADS, P, 3 * P), F32, kind="Internal").ap())
    out = nc.dram_tensor("out_x", (S, D), F32, kind="ExternalOutput").ap()
    args.append(out)
    build(nc, *args)
    r = run_bass_kernel_spmd(nc, [arrays], core_ids=[0])
    return r.results[0]["out_x"].reshape(1, S, D)
```

```python
import math

import numpy as np

import concourse.bass as bass
from concourse import mybir
from contextlib import ExitStack

F32 = mybir.dt.float32
F32R = mybir.dt.float32r
ACT = mybir.ActivationFunctionType
ALU = mybir.AluOpType
AX = mybir.AxisListType

D = 1024
S = 1024
L = 2
P = 128
KT = D // P
NT = S // P
HALF = 512
LOW = 16
DK = 64
DV = 128
CH = 64
HEADS = 4
FF = -(-8 * D // (3 * 256)) * 256
JT = FF // P
W_IN = 3088
C_GQ, C_GK, C_GV, C_GR, C_GA, C_DQ, C_DV = 0, 256, 512, 1024, 1536, 1552, 2576
EPS = 1e-6
BUCKETS, MAX_DIST = 32, 128
MASKED = -3.0e38
NEAR = 2 * P

N_GA, N_GK0, N_WG, N_GK1, N_GQ0, N_GQ1 = range(6)
N_GV = 6
N_GR = N_GV + 4
N_DQK = N_GR + 4
N_DV = N_DQK + 8
N_OUT = N_DV + 4
N_FF = N_OUT + 2 * KT
N_DOWN = N_FF + 2 * JT
SLOTS = N_DOWN + 2 * JT
MODS = 6 * KT
SLOT = KT * P
assert SLOTS % 2 == 0

P_A, P_B, P_G = 0, 8, 16
P_GN, P_DN, P_LAM, P_BG, NPAR = 48, 49, 50, 51, 53
R_BM, R_GAIN, R_REST, NKEPT = 0, MODS, MODS + 4 * KT, MODS + 4 * KT + 5
MOD1 = 2 * KT
MOD2 = MODS - MOD1
MRING = 4
VK = 4

C_ID, C_MASK, C_LAM = 0, P, 2 * P
NCONST = 2 * P + 2 * L
NROW = 2 * (KT * 4) + 2 * L


def layer_constants():
    c = np.zeros((P, NCONST), np.float32)
    j, q = np.arange(P)[:, None], np.arange(P)[None, :]
    c[:, C_ID:C_ID + P] = j == q
    c[:, C_MASK:C_MASK + P] = (j <= q) & (j // CH == q // CH)
    for l in range(L):
        lam = 0.8 - 0.6 * math.exp(-0.3 * l)
        c[:, C_LAM + 2 * l] = lam
        c[:, C_LAM + 2 * l + 1] = 1.0 - lam
    exact = BUCKETS // 2
    hot = np.zeros((BUCKETS + 1, 3 * P), np.float32)
    for at in range(3 * P - 1):
        d = 2 * P - 1 - at
        n = max(d, 0)
        b = n if n < exact else min(BUCKETS - 1, exact + int(
            np.float32(np.log(np.float32(n) / np.float32(exact)))
            / np.float32(math.log(MAX_DIST / exact)) * np.float32(BUCKETS - exact)))
        hot[b, at] += 1.0
        hot[BUCKETS - 1, at] -= 1.0
        if d < 0:
            hot[BUCKETS, at] = 1.0
    return c, hot


def build(nc, x, c, w_mod, b_mod, gains, w_in, w_gate, b_gate, gla_norm, lam_w, diff_norm,
          rel_bias, w_out, w_gu, w_down, consts, onehot, skew, out):
    ctx = ExitStack()
    with ctx:
        def sb(name, shape, dt=F32):
            return ctx.enter_context(nc.sbuf_tensor(name, shape, dt))

        def sem(name):
            return ctx.enter_context(nc.semaphore(name))

        hT = sb("hT", [P, 2, KT, S], F32R)
        wsp = sb("wsp", [P, 2, 2, SLOT], F32R)
        raw = sb("raw", [P, 2, SLOT])
        F = sb("F", [P, JT * S])
        W = sb("W", [P, 5 * 1024])
        cst = sb("cst", [P, NCONST])
        ones = sb("ones", [P, P])
        kept = sb("kept", [P, L, NKEPT])
        cur = sb("cur", [P, NPAR])
        gaT = sb("gaT", [LOW, 2, S], F32R)
        cond = sb("cond", [P, KT])
        mhalf = sb("mhalf", [P, 32])
        st = sb("st", [P, 96])
        ast = sb("ast", [P, 56])
        ps = ctx.enter_context(nc.psum_tensor("ps", [P, 8, 512], F32))
        ident = cst[:, C_ID:C_ID + P]
        gmask = cst[:, C_MASK:C_MASK + P]

        Fq, Fk, Fv, Fg, Fgq, Fgk, Flg = 0, 4096, 8192, 12288, 16384, 18432, 20480
        Fp, Fat, Fbias = 16384, 20480, 21504
        Fx, Fxn, Fv4, Fj = 0, 8192, 16384, 20480
        gb = W[:, 0:1024]
        xt = [W[:, 1024:2048], W[:, 2048:3072]]
        wt = [W[:, 3072:4096], W[:, 4096:5120]]
        diag = W[:, 4096:5120].rearrange("p (k n) -> p k n", k=KT)
        Wd = W[:, 0:256]
        We = [W[:, 256 + 256 * i:512 + 256 * i] for i in range(3)]
        Wqe = [[W[:, 1024 + 512 * r + 256 * z:1280 + 512 * r + 256 * z] for z in range(2)]
               for r in range(2)]
        Wke, Wkd, Wkn = W[:, 2048:2304], W[:, 2304:2560], W[:, 2560:2816]
        Wvt = W[:, 2816:3328]
        Wam = W[:, 3584:4096]
        Wsq = Wam
        Ws = [W[:, 4096 + 256 * i:4352 + 256 * i] for i in range(4)]
        Wq, Wj = [W[:, 0:1024], W[:, 4096:5120]], W[:, 3072:3200]
        Wf = [W[:, 3200 + 32 * z:3232 + 32 * z] for z in range(6)]
        Wmod = W[:, 3392:3392 + MOD2]
        own_ring = [F[:, 4096 + SLOT * z:4096 + SLOT * (z + 1)] for z in range(MRING)]
        own_sum = [F[:, P * q:P * q + P] for q in range(MOD2)]
        next_ring = [F[:, (JT - 2 + z) * S:(JT - 1 + z) * S] for z in range(2)]
        next_sums = W[:, 3072:3072 + MOD1 * P]
        rows_in, lam_in = F[:, 21504:21760], F[:, 21760:22272]
        bias_rows = W[:, 0:HEADS * 3 * P]
        cols, lam_prod = W[:, 1536:1792], W[:, 1792:2048]
        hot, hot_bias, rel = W[:, 2048:2432], W[:, 4480:4992], W[:, 4992:4992 + HEADS]
        mod_first = ([F[:, 8192 + 2048 * z:10240 + 2048 * z] for z in range(6)]
                     + [W[:, 2432:4480], raw.rearrange("p r n -> p (r n)")])
        S_SS, S_MS, S_RS = 0, 24, 48
        S_GSS, S_GMS, S_GRS = 72, 76, 80
        A_NM, A_R, A_RI, A_CO = 0, 16, 32, 48

        s_cst, s_small, s_ones, s_mh = sem("s_cst"), sem("s_small"), sem("s_ones"), sem("s_mh")
        s_xcopy = sem("s_xcopy")
        s_raw = [sem("s_raw0"), sem("s_raw1")]
        s_hi, s_lo = sem("s_hi"), sem("s_lo")
        s_pe = sem("s_pe")
        s_rows, s_cols, s_cond = sem("s_rows"), sem("s_cols"), sem("s_cond")
        s_mf = [sem(f"s_mf{k}") for k in range(KT)]
        s_mfd = sem("s_mfd")
        s_mo = [sem(f"s_mo{r}") for r in range(MRING)]
        s_mn = [sem(f"s_mn{r}") for r in range(2)]
        s_mp, s_ma = sem("s_mp"), sem("s_ma")
        s_mod, s_modv, s_par = sem("s_mod"), sem("s_modv"), sem("s_par")
        s_lp, s_lr, s_le = sem("s_lp"), sem("s_lr"), sem("s_le")
        s_rx, s_rb, s_rbs, s_skew = sem("s_rx"), sem("s_rb"), sem("s_rbs"), sem("s_skew")
        s_cur = sem("s_cur")
        s_bias = sem("s_bias")
        s_xl = [sem(f"s_xl{i}") for i in range(4)]
        s_xr = [sem("s_xr0"), sem("s_xr1")]
        s_n1ss, s_n1ms, s_n1rs = sem("s_n1ss"), sem("s_n1ms"), sem("s_n1rs")
        s_yss, s_yms, s_yrs = sem("s_yss"), sem("s_yms"), sem("s_yrs")
        s_n2ss, s_n2ms, s_n2rs = sem("s_n2ss"), sem("s_n2ms"), sem("s_n2rs")
        s_y, s_yu = sem("s_y"), sem("s_yu")
        s_xs = sem("s_xs")
        s_st = [sem("s_st0"), sem("s_st1")]
        s_xn, s_tr, s_v, s_va = sem("s_xn"), sem("s_tr"), sem("s_v"), sem("s_va")
        s_hh, s_hl = sem("s_hh"), sem("s_hl")
        s_gah, s_gal = sem("s_gah"), sem("s_gal")
        s_zb, s_ab, s_ez, s_ln = sem("s_zb"), sem("s_ab"), sem("s_ez"), sem("s_ln")
        s_lg = sem("s_lg")
        s_tev = sem("s_tev")
        s_nt = sem("s_nt")
        s_gv, s_gr, s_dv = sem("s_gv"), sem("s_gr"), sem("s_dv")
        s_gz = sem("s_gz")
        s_gs0 = sem("s_gs0")
        s_gsc, s_gD, s_gE, s_gC = sem("s_gsc"), sem("s_gD"), sem("s_gE"), sem("s_gC")
        s_gA, s_gd, s_gU, s_gS = sem("s_gA"), sem("s_gd"), sem("s_gU"), sem("s_gS")
        s_gO, s_gsq, s_gss, s_gms = sem("s_gO"), sem("s_gsq"), sem("s_gss"), sem("s_gms")
        s_grs, s_gG, s_gvt = sem("s_grs"), sem("s_gG"), sem("s_gvt")
        s_oT, s_ov = sem("s_oT"), sem("s_ov")
        s_oh, s_ol = sem("s_oh"), sem("s_ol")
        s_qz, s_fin = sem("s_qz"), sem("s_fin")
        s_q, s_qk, s_ba, s_mx = sem("s_q"), sem("s_qk"), sem("s_ba"), sem("s_mx")
        s_ex, s_rc, s_co, s_ad = sem("s_ex"), sem("s_rc"), sem("s_co"), sem("s_ad")
        s_at, s_ate, s_pv = sem("s_at"), sem("s_ate"), sem("s_pv")
        s_asq, s_ams, s_ars, s_on = sem("s_asq"), sem("s_ams"), sem("s_ars"), sem("s_on")
        s_dg, s_gbp, s_gb = sem("s_dg"), sem("s_gbp"), sem("s_gb")
        s_f1, s_f2 = sem("s_f1"), sem("s_f2")
        s_ah, s_al = sem("s_ah"), sem("s_al")
        block = ctx.enter_context(nc.Block())

        CREDIT = 2

        def raw_in(l, n):
            return l * (8 * SLOTS) + 16 * (n // 2 + 1)

        def kn(a):
            return a.rearrange("p (k n) -> p k n", k=KT)

        def tile_of_pairs(base, i, r):
            return F[:, base:base + 2 * S].rearrange("p (a n) -> p a n", a=2)[
                :, :, bass.ds(i * (2 * P) + r * P, P)]

        def head_of_hT(m, h):
            return hT[:, m].rearrange("p k s -> p (k s)")[:, bass.ds(h * S, S)]

        def own_share(m):
            if not 4 <= m < 16:
                return range(0)
            at = (0, 3, 6)[(m - 4) % 3] + (m - 4) // 3 * 8
            return range(at, at + (3, 3, 2)[(m - 4) % 3])

        cond_k = cond[:].unsqueeze(2).to_broadcast([P, KT, P])

        def new_tile(t):
            return xt[t % 2] if t < 4 else F[:, Fx + D * t:Fx + D * t + D]

        def groups_before(b):
            return b + max(0, b - 4)

        xv = out.rearrange("(t p) d -> p t d", p=P)

        def apart(eng):
            eng.nop(nofuse=True)

        @block.sync
        def _(sp):
            sp.dma_start(cst[:], consts).then_inc(s_cst, 16)
            at = 0
            for src in (gains.rearrange("l i (k p) -> (l i k) p", p=P), gla_norm, diff_norm,
                        b_gate.rearrange("l (k p) -> (l k) p", p=P),
                        c.rearrange("b (k p) -> (b k) p", p=P)):
                n = src.shape[0]
                sp.dma_start(rows_in[at:at + n, 0:P], src).then_inc(s_small, 16)
                at += n
            sp.dma_start(rows_in[0:L * MODS, P:2 * P],
                         b_mod.rearrange("l (k p) -> (l k) p", p=P)).then_inc(s_small, 16)
            sp.dma_start(lam_in,
                         lam_w.rearrange("l i d -> (l i d)")[None, :].to_broadcast([P, L * 4 * DK])
                         ).then_inc(s_small, 16)
            sp.dma_start(rel[0:BUCKETS], rel_bias).then_inc(s_small, 16)
            sp.dma_start(hot[0:BUCKETS + 1], onehot).then_inc(s_small, 16)
            mods = w_mod.rearrange("l (k p) c -> p l k c", p=P)
            for k in range(KT):
                sp.dma_start(mod_first[k], mods[:, 0, k, 0:MOD1 * P]).then_inc(s_mf[k], 16)

            for k in range(KT):
                sp.wait_ge(s_mf[k], 16)
            sp.dma_start(out, x).then_inc(s_xcopy, 16)

            sp.wait_ge(s_rbs, HEADS)
            sp.dma_start(skew.rearrange("h q j -> q h j"),
                         bias_rows.rearrange("p (h j) -> p h j", h=HEADS)
                         ).then_inc(s_skew, 16)

            win = w_in.rearrange("l (k p) c -> p l k c", p=P)
            wo = w_out.rearrange("l (k p) c -> p l k c", p=P)
            wgu = w_gu.rearrange("l (k p) c -> p l k c", p=P)
            wdn = w_down.rearrange("l (k p) c -> p l k c", p=P)
            sp.wait_ge(s_mfd, 1)
            with sp.Fori(0, L) as l:
                def load(g, r, dst, src):
                    sp.wait_ge(s_lo, g + 1)
                    apart(sp)
                    sp.dma_start(dst, src).then_inc(s_raw[r], 16)

                def columns(n, c0, w=P):
                    r = n % 2
                    load(l * SLOTS + n, r,
                         raw[:, r, 0:KT * w].rearrange("p (k n) -> p k n", k=KT),
                         win[:, l, :, bass.ds(c0, w)])

                def own_mods(share):
                    for q in share:
                        if q >= MRING:
                            sp.wait_ge(s_mod, l * MODS + q - MRING + 1)
                            apart(sp)
                        sp.dma_start(kn(own_ring[q % MRING]),
                                     mods[:, l, :, (MOD1 + q) * P:(MOD1 + q + 1) * P]
                                     ).then_inc(s_mo[q % MRING], 16)

                def ring_after(n):
                    return [q + MRING for q in own_share(n - 2) if q + MRING < MOD2]

                columns(N_GA, C_GA, LOW)
                columns(N_GK0, C_GK)
                load(l * SLOTS + N_WG, 0, raw[0:LOW, 0, 0:256], w_gate[l])
                columns(N_GK1, C_GK + P)
                sp.wait_ge(s_xn, l * 16 + 8)
                apart(sp)
                own_mods(range(MRING))
                columns(N_GQ0, C_GQ)
                columns(N_GQ1, C_GQ + P)

                def rows4(n0, c0):
                    for i in range(4):
                        n = n0 + i
                        load(l * SLOTS + n, n % 2,
                             raw[:, n % 2, :].rearrange("p (k n) -> p k n", k=2),
                             win[:, l, 2 * i:2 * i + 2, c0:c0 + 512])
                        own_mods(ring_after(n) if n < N_DQK else [])
                rows4(N_GV, C_GV)
                rows4(N_GR, C_GR)
                for i in range(4):
                    for r in range(2):
                        n = N_DQK + 2 * i + r
                        load(l * SLOTS + n, r, kn(raw[:, r, :]),
                             win[:, l, :, C_DQ + (n - N_DQK) * P:C_DQ + (n - N_DQK + 1) * P])
                        own_mods(ring_after(n))
                rows4(N_DV, C_DV)
                for g in range(2):
                    with sp.Fori(0, KT // 2) as i:
                        for r in range(2):
                            load(l * SLOTS + i * 2 + (N_OUT + g * KT + r), r, raw[:, r, :],
                                 wo[:, l, i * 2 + r, :])

                def gate_up(j2, jj):
                    for r in range(2):
                        load(l * SLOTS + j2 * 4 + (N_FF + 2 * jj + r), r, kn(raw[:, r, :]),
                             wgu[:, l, :, bass.ds(j2 * (2 * P) + (jj * P + r * FF), P)])
                with sp.Fori(0, MOD1 // 2) as i:
                    for jj in range(2):
                        gate_up(i, jj)
                        sp.wait_ge(s_n2ss, l * 8 + 8)
                        apart(sp)
                        sp.wait_ge(s_mod, l * MODS + i * 2 + (MOD2 + jj - 1))
                        apart(sp)
                        sp.dma_start(kn(next_ring[jj]),
                                     mods[:, L - 1, :, bass.ds(i * (2 * P) + jj * P, P)]
                                     ).then_inc(s_mn[jj], 16)
                with sp.Fori(MOD1 // 2, JT // 2) as i:
                    for jj in range(2):
                        gate_up(i, jj)
                for g in range(2):
                    with sp.Fori(0, JT // 2) as i:
                        for r in range(2):
                            load(l * SLOTS + i * 2 + (N_DOWN + g * JT + r), r, raw[:, r, :],
                                 wdn[:, l, i * 2 + r, :])

        @block.gpsimd
        def _(pool):
            def load_x(src, pairs):
                for i in pairs:
                    apart(pool)
                    pool.dma_start(F[:, 2048 * i:2048 * i + 2048].rearrange("p (t d) -> p t d", t=2),
                                   src[:, 2 * i:2 * i + 2, :]).then_inc(s_xl[i], 16)

            load_x(x.rearrange("(t p) d -> p t d", p=P), range(4))
            nc.gpsimd.memset(mhalf[:], -0.5).then_inc(s_mh, 1)
            pool.wait_ge(s_mh, 1)
            pool.wait_ge(s_cond, 1)

            def rsqrt(into, frm, w, done):
                nc.gpsimd.tensor_tensor(st[:, into:into + w], st[:, frm:frm + w],
                                        mhalf[:, 0:w], ALU.pow).then_inc(done, 1)

            def mod_product(w):
                nc.gpsimd.tensor_tensor(kn(w), kn(w), cond_k, ALU.mult).then_inc(s_mp, 1)

            def new_x(l, t):
                pool.wait_ge(s_n2ms, l * 8 + t + 1)
                rsqrt(S_RS + 16 + t, S_MS + 16 + t, 1, s_n2rs)
                pool.wait_ge(s_xs, l * 16 + t + 1)
                apart(pool)
                pool.dma_start(xv[:, t, :], F[:, Fx + D * t:Fx + D * t + D]).then_inc(s_st[t % 2], 16)

            def y_root(l, j):
                t = j % NT
                pool.wait_ge(s_yms, l * 16 + j + 1)
                rsqrt(S_RS + 8 + t, S_MS + 8 + t, 1, s_yrs)

            with pool.Fori(0, L) as l:
                for g in range(2):
                    pool.wait_ge(s_n1ms, l * 2 + g + 1)
                    rsqrt(S_RS + 4 * g, S_MS + 4 * g, 4, s_n1rs)
                for q in range(MOD2):
                    pool.wait_ge(s_mo[q % MRING], l * (4 * MOD2) + 16 * (q // MRING + 1))
                    mod_product(own_ring[q % MRING])
                with pool.Fori(0, NT) as t:
                    pool.wait_ge(s_gms, l * NT + t + 1)
                    rsqrt(S_GRS, S_GMS, HEADS, s_grs)
                pool.wait_ge(s_gC, l * NT + NT)
                src = bass.AP(tensor=skew.tensor, offset=skew.offset + P - 1,
                              ap=[[3 * P - 1, P], [P * 3 * P, HEADS], [1, NEAR]])
                apart(pool)
                pool.dma_start(F[:, Fbias:Fbias + HEADS * NEAR].rearrange("p (h k) -> p h k", h=HEADS),
                               src).then_inc(s_bias, 16)
                pool.wait_ge(s_ams, l + 1)
                nc.gpsimd.tensor_tensor(Wf[5], Wf[4], mhalf[:], ALU.pow).then_inc(s_ars, 1)
                pool.wait_ge(s_qk, 1 + l * 64 + 64)
                pool.wait_ge(s_q, l * HEADS + HEADS)
                pool.wait_ge(s_xcopy, 16)
                load_x(xv, range(4))
                for g in range(2):
                    y_root(l, 4 * g)
                    for t in range(4 * g, 4 * g + 4):
                        if t % 4 < 3:
                            y_root(l, t + 1)
                        new_x(l, t)
                with pool.Fori(0, MOD1 // 2) as i:
                    for jj in range(2):
                        pool.wait_ge(s_mn[jj], l * (8 * MOD1) + i * 16 + 16)
                        mod_product(next_ring[jj])
                pool.wait_ge(s_f2, l * JT + JT + CREDIT)
                for t in range(2):
                    apart(pool)
                    pool.dma_start(xt[t], xv[:, t, :]).then_inc(s_xr[t], 16)
                for t in range(NT):
                    if t % 4 == 0:
                        y_root(l, 8 + t)
                    if t % 4 < 3:
                        y_root(l, 8 + t + 1)
                    if t in (1, 2):
                        pool.wait_ge(s_st[t - 1], l * 128 + 64 + 16)
                        apart(pool)
                        pool.dma_start(xt[t - 1], xv[:, t + 1, :]).then_inc(s_xr[t - 1], 16)
                    pool.wait_ge(s_xs, l * 16 + 8 + t + 1)
                    apart(pool)
                    pool.dma_start(xv[:, t, :], new_tile(t)).then_inc(s_st[t % 2], 16)
                    if t == 3:
                        pool.wait_ge(s_al, 1 + l * (2 * JT) + JT + NT)
                        for r in range(2):
                            pool.wait_ge(s_st[r], l * 128 + 96)
                        load_x(xv, range(4))
                for r in range(2):
                    pool.wait_ge(s_st[r], l * 128 + 128)

        @block.scalar
        def _(act):
            def hi(l, n, np_=P, w=SLOT):
                r = n % 2
                act.wait_ge(s_raw[r], raw_in(l, n))
                act.wait_ge(s_pe, l * SLOTS + n + 1)
                nc.scalar.activation(wsp[0:np_, r, 0, 0:w], raw[0:np_, r, 0:w],
                                     ACT.Copy).then_inc(s_hi, 1)

            def hi_dyn(l, n0, i):
                r = n0 % 2
                act.wait_ge(s_raw[r], l * (8 * SLOTS) + i * 16 + 16 * (n0 // 2 + 1))
                act.wait_ge(s_pe, l * SLOTS + i * 2 + (n0 + 1))
                nc.scalar.activation(wsp[:, r, 0, :], raw[:, r, :], ACT.Copy).then_inc(s_hi, 1)

            def hi_ff(l, i, q):
                n0 = N_FF + q + 2
                r = n0 % 2
                act.wait_ge(s_raw[r], l * (8 * SLOTS) + i * 32 + 16 * (n0 // 2 + 1))
                act.wait_ge(s_pe, l * SLOTS + i * 4 + (n0 + 1))
                nc.scalar.activation(wsp[:, r, 0, :], raw[:, r, :], ACT.Copy).then_inc(s_hi, 1)

            def pair(r):
                return ps[:, 2 * r:2 * r + 2, :].rearrange("p a b -> p (a b)")

            act.wait_ge(s_cols, 1)
            nc.scalar.activation(cond[:], cols[:, 72:80], ACT.Silu).then_inc(s_cond, 1)
            act.wait_ge(s_lr, 1)
            nc.scalar.activation(ast[:, 4:8], ast[:, 0:4], ACT.Exp).then_inc(s_le, 1)

            with act.Fori(0, L) as l:
                hi(l, 0, P, KT * LOW)
                hi(l, 1)
                act.wait_ge(s_cur, l + 1)
                for i in range(4):
                    act.wait_ge(s_xl[i], l * 32 + 16)
                    for t in (2 * i, 2 * i + 1):
                        if t:
                            act.wait_ge(s_n1ss, l * 8 + t)
                        nc.scalar.activation(F[:, Fj:Fj + D], F[:, Fx + D * t:Fx + D * t + D],
                                             ACT.Square, accum_out=st[:, S_SS + t:S_SS + t + 1]
                                             ).then_inc(s_n1ss, 1)

                def hT_hi(c0, t):
                    act.wait_ge(s_tr, l * 16 + c0 + t + 1)
                    if t == 0:
                        if c0 == 0:
                            act.wait_ge(s_par, l * 2 + 2)
                    if t >= 4:
                        act.wait_ge(s_hl, l * 16 + c0 + t - 3)
                    a = P_A + (24 if c0 else 0)
                    for k in range(VK, KT):
                        o = Fv4 + D * (t % 4) + P * k
                        last = nc.scalar.activation(F[:, o:o + P], pair(t % 4)[:, P * k:P * k + P],
                                                    ACT.Identity, scale=cur[:, a + k:a + k + 1],
                                                    bias=cur[:, a + KT + k:a + KT + k + 1])
                    last.then_inc(s_va, 1)
                    act.wait_ge(s_va, l * 16 + c0 + t + 1)
                    act.wait_ge(s_v, l * 16 + c0 + t + 1)
                    nc.scalar.activation(hT[:, 0, :, t * P:t * P + P],
                                         F[:, Fv4 + D * (t % 4):Fv4 + D * (t % 4) + D]
                                         .rearrange("p (k n) -> p k n", k=KT),
                                         ACT.Copy).then_inc(s_hh, 1)
                for t in range(NT):
                    hT_hi(0, t)

                act.wait_ge(s_pe, l * SLOTS + 1 + CREDIT)
                hi(l, N_WG, LOW, 256)
                nc.scalar.activation(gaT[:, 0, :], pair(0)[0:LOW], ACT.Copy).then_inc(s_gah, 1)
                for n, dst in ((N_GK0, Fgk), (N_WG, None), (N_GK1, Fgk + S), (N_GQ0, Fgq),
                               (N_GQ1, Fgq + S)):
                    act.wait_ge(s_pe, l * SLOTS + n + 1 + CREDIT)
                    hi(l, n + 2)
                    if dst is not None:
                        b = {N_GK0: 1, N_GK1: 0, N_GQ0: 1, N_GQ1: 0}[n]
                        nc.scalar.activation(F[:, dst:dst + S], pair(b), ACT.Copy).then_inc(s_tev, 1)
                act.wait_ge(s_zb, l * 4 + 4)
                nc.scalar.activation(W[:, 0:2048], F[:, Flg:Flg + 2048], ACT.Abs).then_inc(s_ab, 1)
                act.wait_ge(s_ab, l + 1)
                nc.scalar.activation(W[:, 2048:4096], W[:, 0:2048], ACT.Exp, scale=-1.0
                                     ).then_inc(s_ez, 1)
                act.wait_ge(s_ez, l + 1)
                nc.scalar.activation(W[:, 0:2048], W[:, 2048:4096], ACT.Ln, bias=1.0
                                     ).then_inc(s_ln, 1)
                for n in range(N_GV, N_GV + 4):
                    hi(l, n + 2)
                for n in range(N_GR, N_GR + 4):
                    hi(l, n + 2)
                for t in range(NT):
                    if t < NT - 1:
                        act.wait_ge(s_nt, l * 21 + 7 + t + 1)
                    else:
                        act.wait_ge(s_pe, l * SLOTS + N_GR + 4 + CREDIT)
                    nc.scalar.activation(F[:, Fg + 512 * t:Fg + 512 * t + 512], ps[:, t, :],
                                         ACT.Silu).then_inc(s_gr, 1)

                def gla_exps(i, r, at):
                    act.wait_ge(s_gD, at + 1)
                    C = tile_of_pairs(Flg, i, r)
                    nc.scalar.activation(We[0].rearrange("p (a n) -> p a n", a=2), C, ACT.Exp,
                                         scale=1.0 / 16.0)
                    nc.scalar.activation(We[1].rearrange("p (a n) -> p a n", a=2), C, ACT.Exp,
                                         scale=-1.0 / 16.0)
                    nc.scalar.activation(We[2], Wd, ACT.Exp, scale=-1.0 / 16.0).then_inc(s_gE, 1)

                def gla_tile(i, r, at, more):
                    act.wait_ge(s_gd, at + 1)
                    nc.scalar.activation(Wvt, F[:, bass.ds(i * 1024 + (Fv + r * 512), 512)],
                                         ACT.Copy).then_inc(s_gvt, 1)
                    hi_dyn(l, N_DQK + r + 2, i)
                    nc.scalar.activation(F[:, bass.ds(i * (2 * S) + (Fq + r * S), S)], pair(r),
                                         ACT.Copy).then_inc(s_tev, 1)
                    if more is not None:
                        gla_exps(*more, at + 1)
                    act.wait_ge(s_gO, at + 1)
                    nc.scalar.activation(Wsq, ps[:, 7, :], ACT.Square).then_inc(s_gsq, 1)

                gla_exps(0, 0, l * NT)
                with act.Fori(0, NT // 2 - 1) as i:
                    gla_tile(i, 0, l * NT + i * 2, (i, 1))
                    gla_tile(i, 1, l * NT + i * 2 + 1, (i + 1, 0))
                last2 = NT // 2 - 1
                gla_tile(last2, 0, l * NT + NT - 2, (last2, 1))
                gla_tile(last2, 1, l * NT + NT - 1, None)

                for n in range(N_DV, N_DV + 4):
                    hi(l, n + 2)

                def oT_hi(h, gain):
                    act.wait_ge(s_oT, l * 8 + h + 1)
                    nc.scalar.activation(hT[:, 0, h, :], pair(3 - h % 2), ACT.Copy,
                                         scale=cur[:, gain:gain + 1]).then_inc(s_oh, 1)
                for h in range(HEADS):
                    oT_hi(h, P_GN)

                def counts(h):
                    return l * 64 + h * 16, l * 32 + h * 8, l * 48 + h * 12

                def queries(h):
                    act.wait_ge(s_qk, 1 + counts(h)[0])
                    for m in range(2):
                        rows = slice(DK * m, DK * m + DK)
                        last = nc.scalar.activation(Wq[m][rows], F[rows, bass.ds(h * S + Fq, S)],
                                                    ACT.Copy, scale=DK ** -0.5)
                    last.then_inc(s_q, 1)

                def exps(h, u, after=0):
                    u0, b0, g0 = counts(h)
                    b, m = u // 2, u % 2
                    n = (b + 1) * P
                    act.wait_ge(s_at, 1 + g0 + (groups_before(b - 1) if b >= 2 else after))
                    act.wait_ge(s_mx, u0 + u + 1)
                    at = Fp + 2048 * (b % 2) + 1024 * m
                    nc.scalar.activation(F[:, at:at + n], pair(u % 3)[:, 0:n], ACT.Exp,
                                         bias=ast[:, A_NM + u:A_NM + u + 1],
                                         accum_out=ast[:, A_R + u:A_R + u + 1]
                                         ).then_inc(s_ex, 1)

                def head(h, more):
                    u0, b0, g0 = counts(h)

                    def probs(b, g):
                        j = groups_before(b) + g
                        w = min(512, (b + 1) * P - 512 * g)
                        act.wait_ge(s_at, 1 + g0 + j + 1)
                        act.wait_ge(s_pv, 1 + b0 + b)
                        nc.scalar.activation(F[:, Fat + 512 * g:Fat + 512 * g + w], ps[:, 6, 0:w],
                                             ACT.Copy).then_inc(s_ate, 1)

                    def outs(b):
                        act.wait_ge(s_pv, 1 + b0 + b + 1)
                        act.wait_ge(s_asq, 1 + b0 + b)
                        nc.scalar.activation(Wj, ps[:, 7, 0:DV], ACT.Square,
                                             accum_out=Wf[0][:, bass.ds(h * NT + b, 1)]
                                             ).then_inc(s_asq, 1)
                        nc.scalar.activation(F[:, bass.ds(h * S + (Fg + b * DV), DV)],
                                             ps[:, 7, 0:DV], ACT.Copy).then_inc(s_on, 1)

                    for b in range(NT):
                        probs(b, 0)
                        if 2 * b + 3 < 2 * NT:
                            exps(h, 2 * b + 3)
                        elif more:
                            exps(h + 1, 0, groups_before(NT - 1) - groups_before(NT))
                        if b >= 4:
                            probs(b, 1)
                        if 2 * b + 4 < 2 * NT:
                            exps(h, 2 * b + 4)
                        if b:
                            outs(b - 1)
                        if b == NT - 2 and more:
                            queries(h + 1)
                    if more:
                        exps(h + 1, 1)
                        exps(h + 1, 2)
                    outs(NT - 1)

                act.wait_ge(s_tev, l * 12 + 12)
                act.wait_ge(s_qz, l + 1)
                queries(0)
                for u in range(3):
                    exps(0, u)
                with act.Fori(0, HEADS - 1) as h:
                    head(h, True)
                head(HEADS - 1, False)
                for h in range(HEADS):
                    oT_hi(HEADS + h, P_DN)

                def scratch(ys, xs):
                    act.wait_ge(s_ate, 1 + l * 48 + 48)
                    if ys:
                        act.wait_ge(s_yss, l * 16 + ys)
                    if xs:
                        act.wait_ge(s_n2ss, l * 8 + xs)

                def new_y(j, t, junk):
                    if t % 4 < 3:
                        act.wait_ge(s_y, l * 12 + 3 * (j // 4) + t % 4 + 1)
                    else:
                        end = N_OUT + KT * (j // 4 + 1) if j < 8 else N_DOWN + JT * (j // 4 - 1)
                        act.wait_ge(s_pe, l * SLOTS + end + CREDIT)
                    nc.scalar.activation(junk, pair(t % 4), ACT.Square,
                                         accum_out=st[:, S_SS + 8 + t:S_SS + 9 + t]
                                         ).then_inc(s_yss, 1)

                def new_x(t):
                    act.wait_ge(s_xs, l * 16 + t + 1)
                    nc.scalar.activation(F[:, Fj:Fj + D], F[:, Fx + D * t:Fx + D * t + D],
                                         ACT.Square, accum_out=st[:, S_SS + 16 + t:S_SS + 17 + t]
                                         ).then_inc(s_n2ss, 1)

                for g in range(2):
                    for k in range(KT - 1):
                        hi(l, N_OUT + g * KT + k + 2)
                    for i in range(4):
                        t = 4 * g + i
                        if i == 3:
                            hi(l, N_OUT + g * KT + KT + 1)
                        scratch(t, t if i == 0 else t - 1)
                        new_y(t, t, F[:, Fj:Fj + D])
                        if i:
                            scratch(t + 1, t - 1)
                            new_x(t - 1)
                    scratch(t + 1, t)
                    new_x(t)
                for t in range(NT):
                    hT_hi(8, t)

                with act.Fori(0, JT // 2) as i:
                    for jj in range(2):
                        act.wait_ge(s_pe, l * SLOTS + i * 4 + (N_FF + 2 * jj + 1 + CREDIT))
                        hi_ff(l, i, 2 * jj)
                        act.wait_ge(s_f2, l * JT + i * 2 + (jj + 1))
                        nc.scalar.activation(W[:, 1024 + 1024 * jj:2048 + 1024 * jj],
                                             pair(2 * jj), ACT.Silu).then_inc(s_f1, 1)
                        hi_ff(l, i, 2 * jj + 1)

                def a_hi(g, k, r, count):
                    act.wait_ge(s_pe, count)
                    nc.scalar.activation(hT[:, 0, r, 0:HALF], F[:, k], ACT.Copy
                                         ).then_inc(s_ah, 1)
                act.wait_ge(s_f2, l * JT + JT + CREDIT)
                for r in range(2):
                    a_hi(0, slice(r * S, r * S + HALF), r, l * SLOTS + N_DOWN + CREDIT)
                for g in range(2):
                    with act.Fori(0, JT // 2 - 1) as i:
                        for r in range(2):
                            n0 = N_DOWN + g * JT + r
                            hi_dyn(l, n0 + 2, i)
                            a_hi(g, bass.ds(i * (2 * S) + ((r + 2) * S + g * HALF), HALF), r,
                                 l * SLOTS + i * 2 + (n0 + 1 + CREDIT))
                    def next_half(r):
                        n = N_DOWN + JT - 2 + r
                        hi(l, n + 2)
                        a_hi(1, slice(r * S + HALF, r * S + S), r, l * SLOTS + n + 1 + CREDIT)
                    if g == 0:
                        next_half(0)
                    for i in range(4):
                        t = 4 * g + i
                        if g == 0 and i == 3:
                            next_half(1)
                        scratch(8 + t, 8)
                        new_y(8 + t, t, wt[1])

        @block.vector
        def _(dve):
            v = nc.vector

            def pair(r):
                return ps[:, 2 * r:2 * r + 2, :].rearrange("p a b -> p (a b)")

            def lo(l, n, np_=P, w=SLOT):
                r = n % 2
                dve.wait_ge(s_hi, l * SLOTS + n + 1)
                v.tensor_tensor(wsp[0:np_, r, 1, 0:w], raw[0:np_, r, 0:w],
                                wsp[0:np_, r, 0, 0:w].bitcast(F32), ALU.subtract).then_inc(s_lo, 1)

            def lo_dyn(l, n0, i):
                r = n0 % 2
                dve.wait_ge(s_hi, l * SLOTS + i * 2 + (n0 + 1))
                v.tensor_tensor(wsp[:, r, 1, :], raw[:, r, :], wsp[:, r, 0, :].bitcast(F32),
                                ALU.subtract).then_inc(s_lo, 1)

            def lo_ff(l, i, q):
                n0 = N_FF + q + 2
                r = n0 % 2
                dve.wait_ge(s_hi, l * SLOTS + i * 4 + (n0 + 1))
                v.tensor_tensor(wsp[:, r, 1, :], raw[:, r, :], wsp[:, r, 0, :].bitcast(F32),
                                ALU.subtract).then_inc(s_lo, 1)

            dve.sem_inc(s_lo, CREDIT)
            dve.sem_inc(s_pe, CREDIT)
            dve.sem_inc(s_f2, CREDIT)
            for s in (s_al, s_yu, s_gG, s_ex, s_ate,
                      s_on, s_qk, s_at, s_pv, s_gE, s_asq, s_ol):
                dve.sem_inc(s, 1)
            v.memset(ones[:], 1.0).then_inc(s_ones, 1)
            dve.wait_ge(s_ones, 1)

            dve.wait_ge(s_small, 16 * 9)
            v.memset(rel[BUCKETS:BUCKETS + 1], MASKED).then_inc(s_rx, 1)
            dve.wait_ge(s_rx, 1)
            v.tensor_copy(hot_bias[0:BUCKETS + 1].rearrange("p (h n) -> p h n", h=HEADS),
                          rel[0:BUCKETS + 1].unsqueeze(2)
                          .to_broadcast([BUCKETS + 1, HEADS, P])).then_inc(s_rx, 1)
            dve.wait_ge(s_rows, 1)
            v.tensor_copy(cols[:, 0:80], ps[:, 1, 0:80])
            v.tensor_copy(cols[:, P:P + L * MODS], ps[:, 1, P:P + L * MODS]).then_inc(s_cols, 1)
            dve.wait_ge(s_cols, 1)
            for h in range(HEADS):
                dve.wait_ge(s_rb, h + 1)
                v.tensor_copy(bias_rows[:, 384 * h:384 * h + 384], ps[:, 2 + h, 0:384]
                              ).then_inc(s_rbs, 1)
            lw = lam_in.rearrange("p (a i d) -> p a i d", i=2, d=DK)
            v.tensor_tensor(lam_prod.rearrange("p (a d) -> p a d", a=4), lw[:, :, 0],
                            lw[:, :, 1], ALU.mult).then_inc(s_lp, 1)
            dve.wait_ge(s_lp, 1)
            v.tensor_reduce(ast[:, 0:4], lam_prod.rearrange("p (a d) -> p a d", a=4),
                            AX.X, ALU.add).then_inc(s_lr, 1)
            dve.wait_ge(s_le, 1)
            for l in range(L):
                o = R_REST - P_GN
                v.tensor_copy(kept[:, l, R_BM:R_BM + MODS], cols[:, P + l * MODS:P + (l + 1) * MODS])
                v.tensor_copy(kept[:, l, R_GAIN:R_GAIN + 4 * KT], cols[:, l * 4 * KT:(l + 1) * 4 * KT])
                v.scalar_tensor_tensor(kept[:, l, o + P_LAM:o + P_LAM + 1],
                                       ast[:, 4 + 2 * l + 1:4 + 2 * l + 2],
                                       cst[:, C_LAM + 2 * l:C_LAM + 2 * l + 1],
                                       ast[:, 4 + 2 * l:4 + 2 * l + 1], ALU.subtract, ALU.subtract)
                v.tensor_copy(kept[:, l, o + P_GN:o + P_GN + 1], cols[:, 64 + l:65 + l])
                v.tensor_scalar(kept[:, l, o + P_DN:o + P_DN + 1], cols[:, 66 + l:67 + l],
                                cst[:, C_LAM + 2 * l + 1:C_LAM + 2 * l + 2], None, ALU.mult)
                last = v.tensor_copy(kept[:, l, o + P_BG:o + P_BG + 2],
                                     cols[:, 68 + 2 * l:70 + 2 * l])
            last.then_inc(s_par, 1)
            dve.wait_ge(s_par, 1)

            def norm_columns(s, m, gain):
                v.tensor_copy(cur[:, 24 * s + P_B:24 * s + P_B + KT], m[:, 0:KT])
                return v.scalar_tensor_tensor(cur[:, 24 * s + P_A:24 * s + P_A + KT],
                                              m[:, KT:2 * KT], 1.0, gain, ALU.add, ALU.mult)

            dve.wait_ge(s_mfd, 1)
            v.tensor_tensor(Wmod[:, 0:MOD1], ps[:, 0, 0:MOD1], kept[:, 0, R_BM:R_BM + MOD1],
                            ALU.add).then_inc(s_modv, 1)
            dve.wait_ge(s_modv, 1)
            norm_columns(0, Wmod, kept[:, 0, R_GAIN:R_GAIN + KT]).then_inc(s_par, 1)
            dve.wait_ge(s_skew, 16)
            dve.wait_ge(s_par, 2)

            with dve.Fori(0, L) as l:
                v.tensor_copy(cur[:, P_GN:NPAR], kept[:, l, R_REST:NKEPT]).then_inc(s_cur, 1)
                lo(l, 0, P, KT * LOW)
                lo(l, 1)
                for t in range(NT):
                    if t % 4 == 0:
                        dve.wait_ge(s_n1ss, l * 8 + t + 4)
                        v.tensor_scalar(st[:, S_MS + t:S_MS + t + 4], st[:, S_SS + t:S_SS + t + 4],
                                        1.0 / D, EPS, ALU.mult, ALU.add).then_inc(s_n1ms, 1)
                        dve.wait_ge(s_n1rs, l * 2 + t // 4 + 1)
                    v.tensor_scalar(F[:, Fxn + D * t:Fxn + D * t + D], F[:, Fx + D * t:Fx + D * t + D],
                                    st[:, S_RS + t:S_RS + t + 1], None, ALU.mult).then_inc(s_xn, 1)
                dve.wait_ge(s_cur, l + 1)

                def hT_v(c0, t):
                    dve.wait_ge(s_tr, l * 16 + c0 + t + 1)
                    a = P_A + (24 if c0 else 0)
                    for k in range(VK):
                        o = Fv4 + D * (t % 4) + P * k
                        last = v.tensor_scalar(F[:, o:o + P], pair(t % 4)[:, P * k:P * k + P],
                                               cur[:, a + k:a + k + 1], cur[:, a + KT + k:a + KT + k + 1],
                                               ALU.mult, ALU.add)
                    last.then_inc(s_v, 1)

                def hT_lo(c0, t):
                    dve.wait_ge(s_hh, l * 16 + c0 + t + 1)
                    v.tensor_tensor(hT[:, 1, :, t * P:t * P + P],
                                    kn(F[:, Fv4 + D * (t % 4):Fv4 + D * (t % 4) + D]),
                                    hT[:, 0, :, t * P:t * P + P].bitcast(F32),
                                    ALU.subtract).then_inc(s_hl, 1)

                def norm_out(c0):
                    for t in range(NT + 1):
                        if t < NT:
                            hT_v(c0, t)
                        if t:
                            hT_lo(c0, t - 1)
                norm_out(0)

                def lo_sums(m):
                    lo(l, m)
                    for q in own_share(m):
                        dve.wait_ge(s_mp, l * MODS + q + 1)
                        v.tensor_reduce(own_sum[q], own_ring[q % MRING].rearrange(
                            "p (k n) -> p n k", k=KT), AX.X, ALU.add).then_inc(s_mod, 1)

                lo(l, N_WG, LOW, 256)
                dve.wait_ge(s_gah, l + 1)
                v.tensor_tensor(gaT[:, 1, :], pair(0)[0:LOW], gaT[:, 0, :].bitcast(F32),
                                ALU.subtract).then_inc(s_gal, 1)
                lo_sums(N_GK0 + 2)
                lo_sums(N_WG + 2)
                for i in range(4):
                    o = Flg + 512 * i
                    v.tensor_scalar(F[:, o:o + 512], ps[:, 4 + i, :],
                                    cur[:, P_BG + i // 2:P_BG + i // 2 + 1], None,
                                    ALU.add).then_inc(s_zb, 1)
                lo_sums(N_GK1 + 2)
                lo_sums(N_GQ0 + 2)
                lo_sums(N_GQ1 + 2)
                dve.wait_ge(s_ln, l + 1)
                v.scalar_tensor_tensor(F[:, Flg:Flg + 2048], F[:, Flg:Flg + 2048], 0.0,
                                       W[:, 0:2048], ALU.min, ALU.subtract).then_inc(s_lg, 1)
                for n in range(N_GV, N_GV + 4):
                    lo_sums(n + 2)
                for t in range(NT):
                    if t < NT - 1:
                        dve.wait_ge(s_nt, l * 21 + t + 1)
                    else:
                        dve.wait_ge(s_pe, l * SLOTS + N_GV + 4 + CREDIT)
                    v.tensor_copy(F[:, Fv + 512 * t:Fv + 512 * t + 512], ps[:, t, :]
                                  ).then_inc(s_gv, 1)
                for n in range(N_GR, N_GR + 4):
                    lo_sums(n + 2)

                dve.wait_ge(s_lg, l + 1)
                v.memset(W[:, 1024:2048], 0.0).then_inc(s_gz, 1)
                v.memset(Ws[0], 0.0).then_inc(s_gs0, 1)
                dve.wait_ge(s_gz, l + 1)
                apart(dve)

                def gla_gates(i, r, at):
                    for p in range(2):
                        for e in range(2):
                            cc = F[:, bass.ds(i * (2 * P) + (Flg + p * S + r * P + e * CH), CH)]
                            last = v.tensor_tensor_scan(cc, ones[:, 0:CH], cc, 0.0,
                                                        ALU.mult, ALU.add)
                    last.then_inc(s_gsc, 1)
                    dve.wait_ge(s_gsc, at + 1)
                    dve.wait_ge(s_gE, 1 + at)
                    for p in range(2):
                        Cp = F[:, bass.ds(i * (2 * P) + (Flg + p * S + r * P), P)].rearrange(
                            "p (e n) -> p e n", e=2)
                        last = v.tensor_tensor(
                            Wd[:, p * P:p * P + P].rearrange("p (e n) -> p e n", e=2), Cp,
                            Cp[:, :, CH - 1:CH].to_broadcast([P, 2, CH]), ALU.subtract)
                    last.then_inc(s_gD, 1)
                    dve.wait_ge(s_gE, 1 + at + 1)
                    q = tile_of_pairs(Fgq, i, r)
                    k = tile_of_pairs(Fgk, i, r)
                    a2 = lambda z: z.rearrange("p (a n) -> p a n", a=2)
                    for z in range(2):
                        own = slice(DK * z, DK * z + DK)
                        v.scalar_tensor_tensor(a2(Wqe[r][z])[own], q[own], DK ** -0.5,
                                               a2(We[0])[own], ALU.mult, ALU.mult)
                    v.tensor_tensor(a2(Wke), k, a2(We[1]), ALU.mult)
                    v.tensor_tensor(a2(Wkd), k, a2(We[2]), ALU.mult).then_inc(s_gC, 1)

                def gla_tile(i, r, at, more):
                    dve.wait_ge(s_gA, at + 1)
                    v.tensor_copy(Wkn, ps[:, 4, 0:256])
                    v.tensor_tensor(Wam.rearrange("p (h n) -> p h n", h=HEADS),
                                    ps[:, 5, :].rearrange("p (h n) -> p h n", h=HEADS),
                                    gmask.unsqueeze(1).to_broadcast([P, HEADS, P]),
                                    ALU.mult).then_inc(s_gd, 1)
                    lo_dyn(l, N_DQK + r + 2, i)
                    dve.wait_ge(s_gU, at + 1)
                    for e in range(2):
                        for p in range(2):
                            src, dst = Ws[2 * r + e], Ws[(2 * r + e + 1) % 4]
                            d = We[0][:, p * P + e * CH + CH - 1:p * P + e * CH + CH]
                            last = v.scalar_tensor_tensor(
                                dst[:, p * P:p * P + P], src[:, p * P:p * P + P], d,
                                ps[:, 6 - 2 * e, p * P:p * P + P], ALU.mult, ALU.add)
                        last.then_inc(s_gS, 1)
                        dve.wait_ge(s_gS, at * 2 + (e + 1))
                    if more is not None:
                        gla_gates(*more, at + 1)
                    dve.wait_ge(s_gsq, at + 1)
                    v.tensor_reduce(st[:, S_GSS:S_GSS + 4], Wsq.rearrange("p (h n) -> p h n", h=4),
                                    AX.X, ALU.add).then_inc(s_gss, 1)
                    dve.wait_ge(s_gss, at + 1)
                    v.tensor_scalar(st[:, S_GMS:S_GMS + 4], st[:, S_GSS:S_GSS + 4], 1.0 / DV, EPS,
                                    ALU.mult, ALU.add).then_inc(s_gms, 1)
                    dve.wait_ge(s_grs, at + 1)
                    for h in range(HEADS):
                        o = F[:, bass.ds(i * 1024 + (Fg + r * 512 + h * DV), DV)]
                        last = v.scalar_tensor_tensor(
                            o, ps[:, 7, h * DV:(h + 1) * DV], st[:, S_GRS + h:S_GRS + h + 1], o,
                            ALU.mult, ALU.mult)
                    last.then_inc(s_gG, 1)

                dve.wait_ge(s_gs0, l + 1)
                gla_gates(0, 0, l * NT)
                dve.wait_ge(s_ma, l * 2 + 1)
                v.tensor_tensor(Wmod[:, 0:MOD2], ps[:, 7, 0:MOD2], kept[:, l, R_BM + MOD1:R_BM + MODS],
                                ALU.add).then_inc(s_modv, 1)
                dve.wait_ge(s_modv, l * 2 + 2)
                gains_l = kept[:, l, R_GAIN:R_GAIN + 4 * KT]
                v.tensor_tensor(cur[:, P_G:P_G + KT], Wmod[:, 0:KT], gains_l[:, KT:2 * KT],
                                ALU.mult)
                norm_columns(1, Wmod[:, KT:3 * KT], gains_l[:, 2 * KT:3 * KT])
                v.tensor_tensor(cur[:, 24 + P_G:24 + P_G + KT], Wmod[:, 3 * KT:4 * KT],
                                gains_l[:, 3 * KT:4 * KT], ALU.mult).then_inc(s_par, 1)
                dve.wait_ge(s_par, l * 2 + 3)
                apart(dve)
                with dve.Fori(0, NT // 2 - 1) as i:
                    gla_tile(i, 0, l * NT + i * 2, (i, 1))
                    gla_tile(i, 1, l * NT + i * 2 + 1, (i + 1, 0))
                last2 = NT // 2 - 1
                gla_tile(last2, 0, l * NT + NT - 2, (last2, 1))
                gla_tile(last2, 1, l * NT + NT - 1, None)

                for n in range(N_DV, N_DV + 4):
                    lo(l, n + 2)
                for t in range(NT):
                    if t < NT - 1:
                        dve.wait_ge(s_nt, l * 21 + 14 + t + 1)
                    else:
                        dve.wait_ge(s_pe, l * SLOTS + N_DV + 4 + CREDIT)
                    v.tensor_copy(F[:, Fv + 512 * t:Fv + 512 * t + 512], ps[:, t, :]
                                  ).then_inc(s_dv, 1)

                def oT_lo(h, gain):
                    dve.wait_ge(s_oh, l * 8 + h + 1)
                    v.scalar_tensor_tensor(hT[:, 1, h, :], pair(3 - h % 2), cur[:, gain:gain + 1],
                                           hT[:, 0, h, :].bitcast(F32), ALU.mult,
                                           ALU.subtract).then_inc(s_ol, 1)
                for h in range(HEADS):
                    oT_lo(h, P_GN)

                v.memset(Wq[0][DK:P], 0.0)
                v.memset(Wq[1][0:DK], 0.0).then_inc(s_qz, 1)
                dve.wait_ge(s_bias, l * 16 + 16)
                apart(dve)
                def maxes(h, u):
                    u0 = l * 64 + h * 16
                    n = (u // 2 + 1) * P
                    w = min(n, NEAR)
                    dve.wait_ge(s_qk, 1 + u0 + u + 1)
                    near = pair(u % 3)[:, n - w:n]
                    v.tensor_tensor(near, near, F[:, bass.ds(h * NEAR + (Fbias + NEAR - w), w)],
                                    ALU.add).then_inc(s_ba, 1)
                    dve.wait_ge(s_ba, u0 + u + 1)
                    v.tensor_reduce(ast[:, A_NM + u:A_NM + u + 1], pair(u % 3)[:, 0:n], AX.X,
                                    ALU.max, negate=True).then_inc(s_mx, 1)

                def head(h, more):
                    u0 = l * 64 + h * 16
                    b0 = l * 32 + h * 8

                    def combine(b):
                        n, i = (b + 1) * P, 2 * b
                        dve.wait_ge(s_ex, 1 + u0 + i + 2)
                        v.reciprocal(ast[:, A_RI + i + 1:A_RI + i + 2], ast[:, A_R + i + 1:A_R + i + 2]
                                     ).then_inc(s_rc, 1)
                        v.tensor_copy(Wf[1][:, bass.ds(h * NT + b, 1)], ast[:, A_R + i:A_R + i + 1])
                        dve.wait_ge(s_rc, b0 + b + 1)
                        v.tensor_scalar(ast[:, A_CO + b:A_CO + b + 1], ast[:, A_R + i:A_R + i + 1],
                                        ast[:, A_RI + i + 1:A_RI + i + 2], cur[:, P_LAM:P_LAM + 1],
                                        ALU.mult, ALU.mult).then_inc(s_co, 1)
                        dve.wait_ge(s_co, b0 + b + 1)
                        p0 = F[:, Fp + 2048 * (b % 2):Fp + 2048 * (b % 2) + n]
                        p1 = F[:, Fp + 2048 * (b % 2) + 1024:Fp + 2048 * (b % 2) + 1024 + n]
                        v.scalar_tensor_tensor(p0, p1, ast[:, A_CO + b:A_CO + b + 1], p0,
                                               ALU.mult, ALU.add).then_inc(s_ad, 1)

                    for b in range(NT):
                        combine(b)
                        for u in (2 * b + 3, 2 * b + 4):
                            if u < 2 * NT:
                                maxes(h, u)
                    if more:
                        for u in range(3):
                            maxes(h + 1, u)

                for u in range(3):
                    maxes(0, u)
                apart(dve)
                with dve.Fori(0, HEADS - 1) as h:
                    head(h, True)
                head(HEADS - 1, False)

                def gate_diagonals(s):
                    for k in range(KT):
                        a = P_G + 24 * s + k
                        last = v.tensor_scalar(diag[:, k, :], ident, cur[:, a:a + 1], None, ALU.mult)
                    last.then_inc(s_dg, 1)

                def gate_row(s):
                    dve.wait_ge(s_gbp, l * 2 + s + 1)
                    v.tensor_copy(gb, pair(0)).then_inc(s_gb, 1)

                dve.wait_ge(s_on, 1 + l * 32 + 32)
                dve.wait_ge(s_ad, l * 32 + 32)
                v.reciprocal(Wf[2], Wf[1]).then_inc(s_fin, 1)
                dve.wait_ge(s_fin, l * 4 + 1)
                v.tensor_tensor(Wf[3], Wf[0], Wf[2], ALU.mult).then_inc(s_fin, 1)
                dve.wait_ge(s_fin, l * 4 + 2)
                v.tensor_tensor(Wf[3], Wf[3], Wf[2], ALU.mult).then_inc(s_fin, 1)
                dve.wait_ge(s_fin, l * 4 + 3)
                v.tensor_scalar(Wf[4], Wf[3], 1.0 / DV, EPS, ALU.mult, ALU.add).then_inc(s_ams, 1)
                gate_diagonals(0)
                dve.wait_ge(s_ars, l + 1)
                v.tensor_tensor(Wf[3], Wf[5], Wf[2], ALU.mult).then_inc(s_fin, 1)
                dve.wait_ge(s_fin, l * 4 + 4)
                for h in range(HEADS):
                    o = F[:, Fg + S * h:Fg + S * h + S].rearrange("p (b n) -> p b n", b=NT)
                    v.tensor_tensor(o, o, Wf[3][:, NT * h:NT * h + NT].unsqueeze(2)
                                    .to_broadcast([P, NT, DV]), ALU.mult).then_inc(s_ov, 1)
                gate_row(0)
                for h in range(HEADS):
                    oT_lo(HEADS + h, P_DN)

                def y_mean(j, t):
                    dve.wait_ge(s_yss, l * 16 + j + 1)
                    v.tensor_scalar(st[:, S_MS + 8 + t:S_MS + 9 + t], st[:, S_SS + 8 + t:S_SS + 9 + t],
                                    1.0 / D, EPS, ALU.mult, ALU.add).then_inc(s_yms, 1)

                def y_add(j, t, tmp, old, new):
                    dve.wait_ge(s_yrs, l * 16 + j + 1)
                    if j >= 1:
                        dve.wait_ge(s_xs, l * 16 + j)
                    v.scalar_tensor_tensor(tmp, pair(t % 4), st[:, S_RS + 8 + t:S_RS + 9 + t], gb,
                                           ALU.mult, ALU.mult).then_inc(s_yu, 1)
                    dve.wait_ge(s_yu, 1 + l * 16 + j + 1)
                    v.tensor_tensor(new, old, tmp, ALU.add).then_inc(s_xs, 1)

                def x_norm(t):
                    dve.wait_ge(s_n2ss, l * 8 + t + 1)
                    v.tensor_scalar(st[:, S_MS + 16 + t:S_MS + 17 + t],
                                    st[:, S_SS + 16 + t:S_SS + 17 + t],
                                    1.0 / D, EPS, ALU.mult, ALU.add).then_inc(s_n2ms, 1)
                    dve.wait_ge(s_n2rs, l * 8 + t + 1)
                    v.tensor_scalar(F[:, Fxn + D * t:Fxn + D * t + D], F[:, Fx + D * t:Fx + D * t + D],
                                    st[:, S_RS + 16 + t:S_RS + 17 + t], None, ALU.mult
                                    ).then_inc(s_xn, 1)

                dve.wait_ge(s_gb, l * 2 + 1)
                for g in range(2):
                    for k in range(KT - 1):
                        lo(l, N_OUT + g * KT + k + 2)
                    y_mean(4 * g, 4 * g)
                    for i in range(4):
                        t = 4 * g + i
                        if i == 2:
                            lo(l, N_OUT + g * KT + KT + 1)
                        if i < 3:
                            y_mean(t + 1, t + 1)
                        dve.wait_ge(s_xl[t // 2], l * 32 + 32)
                        x_t = F[:, Fx + D * t:Fx + D * t + D]
                        y_add(t, t, wt[t % 2], x_t, x_t)
                        if i:
                            x_norm(t - 1)
                    x_norm(4 * g + 3)
                norm_out(8)

                for r in range(2):
                    dve.wait_ge(s_st[r], l * 128 + 64)
                apart(dve)
                def gate_up(i, jj):
                    lo_ff(l, i, 2 * jj)
                    lo_ff(l, i, 2 * jj + 1)
                    dve.wait_ge(s_f1, l * JT + i * 2 + (jj + 1))
                    dve.wait_ge(s_pe, l * SLOTS + i * 4 + (N_FF + 2 * jj + 2 + CREDIT))
                    v.tensor_tensor(F[:, bass.ds(i * 2048 + jj * 1024, 1024)],
                                    W[:, 1024 + 1024 * jj:2048 + 1024 * jj], pair(2 * jj + 1),
                                    ALU.mult).then_inc(s_f2, 1)
                with dve.Fori(0, MOD1 // 2) as i:
                    for jj in range(2):
                        gate_up(i, jj)
                        dve.wait_ge(s_mp, l * MODS + i * 2 + (MOD2 + jj + 1))
                        v.tensor_reduce(next_sums[:, bass.ds(i * (2 * P) + jj * P, P)],
                                        next_ring[jj].rearrange("p (k n) -> p n k", k=KT),
                                        AX.X, ALU.add).then_inc(s_mod, 1)
                dve.wait_ge(s_mod, l * MODS + MODS)
                apart(dve)
                with dve.Fori(MOD1 // 2, JT // 2) as i:
                    for jj in range(2):
                        gate_up(i, jj)
                dve.wait_ge(s_ma, l * 2 + 2)
                v.tensor_tensor(Wmod[:, 0:MOD1], ps[:, 2, 0:MOD1], kept[:, L - 1, R_BM:R_BM + MOD1],
                                ALU.add).then_inc(s_modv, 1)
                dve.wait_ge(s_modv, l * 2 + 3)
                norm_columns(0, Wmod, kept[:, L - 1, R_GAIN:R_GAIN + KT]).then_inc(s_par, 1)
                dve.wait_ge(s_par, l * 2 + 4)

                gate_diagonals(1)
                gate_row(1)
                dve.wait_ge(s_gb, l * 2 + 2)

                def a_lo(src, r, count):
                    dve.wait_ge(s_ah, count)
                    v.tensor_tensor(hT[:, 1, r, 0:HALF], F[:, src], hT[:, 0, r, 0:HALF].bitcast(F32),
                                    ALU.subtract).then_inc(s_al, 1)
                for r in range(2):
                    a_lo(slice(r * S, r * S + HALF), r, l * (2 * JT) + r + 1)
                for g in range(2):
                    with dve.Fori(0, JT // 2 - 1) as i:
                        for r in range(2):
                            lo_dyn(l, N_DOWN + g * JT + r + 2, i)
                            a_lo(bass.ds(i * (2 * S) + ((r + 2) * S + g * HALF), HALF), r,
                                 l * (2 * JT) + i * 2 + (g * JT + r + 3))
                    def next_half(r):
                        lo(l, N_DOWN + JT + r)
                        a_lo(slice(r * S + HALF, r * S + S), r, l * (2 * JT) + JT + r + 1)
                    if g == 0:
                        next_half(0)
                    y_mean(8 + 4 * g, 4 * g)
                    for i in range(4):
                        t = 4 * g + i
                        if g == 0 and i == 2:
                            next_half(1)
                        if i < 3:
                            y_mean(8 + t + 1, t + 1)
                        if t < 4:
                            dve.wait_ge(s_xr[t % 2], l * 32 + 16 * (t // 2 + 1))
                        else:
                            dve.wait_ge(s_xl[t // 2], l * 32 + 48)
                        y_add(8 + t, t, wt[0], new_tile(t), new_tile(t))
                dve.wait_ge(s_xs, l * 16 + 16)

        @block.tensor
        def _(pe):
            mm = nc.tensor.matmul

            def pair(r):
                return ps[:, 2 * r:2 * r + 2, :].rearrange("p a b -> p (a b)")

            def three(o, a, b, start, stop):
                mm(o, a(0), b(0), start=start, stop=False)
                mm(o, a(0), b(1), start=False, stop=False)
                return mm(o, a(1), b(0), start=False, stop=stop)

            pe.wait_ge(s_cst, 16)
            pe.wait_ge(s_small, 16 * 9)
            nc.tensor.transpose(ps[:, 1, 0:80], rows_in[0:80, 0:P], ident[0:80, 0:80])
            nc.tensor.transpose(ps[:, 1, P:P + L * MODS], rows_in[0:L * MODS, P:2 * P],
                                ident[0:L * MODS, 0:L * MODS]).then_inc(s_rows, 1)
            pe.wait_ge(s_rx, 2)
            for h in range(HEADS):
                mm(ps[:, 2 + h, 0:3 * P], hot_bias[0:BUCKETS + 1, P * h:P * h + P],
                   hot[0:BUCKETS + 1], start=True, stop=True).then_inc(s_rb, 1)
            pe.wait_ge(s_cond, 1)
            for k in range(KT):
                pe.wait_ge(s_mf[k], 16)
                for j in range(MOD1):
                    last = mm(ps[:, 0, j:j + 1], mod_first[k][:, j * P:j * P + P],
                              cond[:, k:k + 1],
                              start=(k == 0 and j == 0), stop=(k == KT - 1),
                              skip_group_check=True)
            last.then_inc(s_mfd, 1)
            pe.wait_ge(s_ones, 1)
            pe.wait_ge(s_modv, 1)

            with pe.Fori(0, L) as l:
                def split(n):
                    pe.wait_ge(s_lo, l * SLOTS + n + 1 + CREDIT)

                def norm_tr(c0, t):
                    pe.wait_ge(s_xn, l * 16 + c0 + t + 1)
                    if t >= 4:
                        pe.wait_ge(s_v, l * 16 + c0 + t - 3)
                        pe.wait_ge(s_va, l * 16 + c0 + t - 3)
                    elif c0:
                        pe.wait_ge(s_yu, 1 + l * 16 + 4 + t + 1)
                    else:
                        pe.wait_ge(s_yu, 1 + l * 16)
                    for k in range(KT):
                        o = Fxn + D * t + P * k
                        last = nc.tensor.transpose(pair(t % 4)[:, P * k:P * k + P], F[:, o:o + P], ident)
                    last.then_inc(s_tr, 1)

                for t in range(NT):
                    norm_tr(0, t)

                def columns(n_parity, b, halves=(0, 1), w=P, m=P):
                    r = n_parity
                    for hf in halves:
                        for k in range(KT):
                            last = three(pair(b)[0:m, HALF * hf:HALF * hf + HALF],
                                         lambda z: wsp[:, r, z, k * w:k * w + w],
                                         lambda z: hT[:, z, k, HALF * hf:HALF * hf + HALF],
                                         k == 0, k == KT - 1)
                    return last

                def halves_in_turn(c0, first, second):
                    for hf in range(2):
                        pe.wait_ge(s_hl, l * 16 + c0 + 4 * hf + 4)
                        for b, slot in enumerate((first, second)):
                            pe.wait_ge(s_v, l * 16 + c0 + 5 + b)
                            pe.wait_ge(s_va, l * 16 + c0 + 5 + b)
                            last = slot(hf)
                            if hf:
                                last.then_inc(s_pe, 1)

                def low_rank(hf):
                    split(N_GA)
                    return columns(0, 0, (hf,), w=LOW, m=LOW)

                def first_key(hf):
                    split(N_GK0)
                    return columns(1, 1, (hf,))
                halves_in_turn(0, low_rank, first_key)
                split(N_WG)
                pe.wait_ge(s_gal, l + 1)
                for i in range(4):
                    p, hf = i // 2, i % 2
                    last = three(ps[:, 4 + i, :], lambda z: wsp[0:LOW, 0, z, p * P:p * P + P],
                                 lambda z: gaT[:, z, hf * HALF:hf * HALF + HALF], True, True)
                last.then_inc(s_pe, 1)
                split(N_GK1)
                columns(1, 0).then_inc(s_pe, 1)
                split(N_GQ0)
                pe.wait_ge(s_tev, l * 12 + 1)
                columns(0, 1).then_inc(s_pe, 1)
                split(N_GQ1)
                pe.wait_ge(s_tev, l * 12 + 2)
                columns(1, 0).then_inc(s_pe, 1)

                def rows(n0, free):
                    for i in range(4):
                        n = n0 + i
                        split(n)
                        for t in range(NT):
                            if i == 0:
                                free(t)
                            for kk in range(2):
                                k = 2 * i + kk
                                last = three(ps[:, t, :], lambda z: hT[:, z, k, t * P:t * P + P],
                                             lambda z: wsp[:, n % 2, z, kk * 512:kk * 512 + 512],
                                             k == 0, k == KT - 1)
                            if i == 3 and t < NT - 1:
                                last.then_inc(s_nt, 1)
                        last.then_inc(s_pe, 1)

                def free_gv(t):
                    pe.wait_ge(s_tev, l * 12 + 4)
                    pe.wait_ge(s_zb, l * 4 + 4)
                rows(N_GV, free_gv)
                rows(N_GR, lambda t: pe.wait_ge(s_gv, l * 8 + t + 1))

                pe.wait_ge(s_gr, l * 8 + 8)
                pe.wait_ge(s_mod, l * MODS + MOD2)
                for q in range(MOD2):
                    last = mm(ps[:, 7, q:q + 1], own_sum[q], ones[:, 0:1], start=True, stop=True)
                last.then_inc(s_ma, 1)
                apart(pe)
                with pe.Fori(0, NT // 2) as i:
                    for r in range(2):
                        at = l * NT + i * 2 + r
                        n = N_DQK + r
                        pe.wait_ge(s_lo, l * SLOTS + i * 2 + (n + 1 + CREDIT))
                        pe.wait_ge(s_tev, l * 12 + i * 2 + (4 + r - 1))
                        columns(r, r, (0,))
                        pe.wait_ge(s_gC, at + 1)
                        for p in range(2):
                            nc.tensor.transpose(ps[:, 4, p * P:p * P + P], Wkd[:, p * P:p * P + P],
                                                ident)
                        for h in range(HEADS):
                            p, b = h // 2, DK * (h % 2)
                            last = mm(ps[:, 5, h * P:h * P + P], Wke[:, p * P:p * P + P],
                                      Wqe[r][h % 2][:, p * P:p * P + P], start=True, stop=True)
                        last.then_inc(s_gA, 1)
                        columns(r, r, (1,)).then_inc(s_pe, 1)
                        pe.wait_ge(s_gd, at + 1)
                        pe.wait_ge(s_gvt, at + 1)
                        apart(pe)
                        for e in range(2):
                            for h in range(HEADS):
                                p, b = h // 2, DK * (h % 2)
                                vv = Wvt[e * CH:e * CH + CH, h * DV:h * DV + DV]
                                last = mm(ps[b:b + DK, 6 - 2 * e, p * P:p * P + P],
                                          Wkn[e * CH:e * CH + CH, p * P + b:p * P + b + DK], vv,
                                          start=True, stop=True)
                        last.then_inc(s_gU, 1)
                        pe.wait_ge(s_gG, 1 + at)
                        for h in range(HEADS):
                            mm(ps[:, 7, h * DV:(h + 1) * DV], Wam[:, h * P:h * P + P],
                               Wvt[:, h * DV:h * DV + DV], start=(h == 0), stop=False,
                               skip_group_check=True)
                        pe.wait_ge(s_gS, at * 2 + 1)
                        for h in range(HEADS):
                            p = h // 2
                            o = ps[:, 7, h * DV:(h + 1) * DV]
                            for e in range(2):
                                last = mm(o[e * CH:e * CH + CH],
                                          Wqe[r][h % 2][:, p * P + e * CH:p * P + e * CH + CH],
                                          Ws[2 * r + e][:, p * P:p * P + P],
                                          start=False, stop=(e == 1), skip_group_check=True)
                        last.then_inc(s_gO, 1)

                pe.wait_ge(s_gG, 1 + l * NT + NT)
                pe.wait_ge(s_tev, l * 12 + 12)
                rows(N_DV, lambda t: None)

                def to_features(h, src):
                    if h % HEADS >= 2:
                        pe.wait_ge(s_ol, 1 + l * 8 + h - 1)
                    for t in range(NT):
                        last = nc.tensor.transpose(pair(3 - h % 2)[:, t * P:t * P + P], src(t), ident)
                    last.then_inc(s_oT, 1)
                pe.wait_ge(s_dv, l * 8 + 8)
                for h in range(HEADS):
                    to_features(h, lambda t: F[:, Fg + 512 * t + DV * h:Fg + 512 * t + DV * h + DV])
                pe.wait_ge(s_ol, 1 + l * 8 + 4)
                apart(pe)

                def scores(h, u):
                    u0 = l * 64 + h * 16
                    b, m = u // 2, u % 2
                    n = (b + 1) * P
                    pe.wait_ge(s_ex, 1 + u0 + max(0, u - 2))
                    for c0 in range(0, n, 512):
                        w = min(512, n - c0)
                        last = mm(pair(u % 3)[:, c0:c0 + w], Wq[m][:, b * P:b * P + P],
                                  F[:, bass.ds(h * S + (Fk + c0), w)],
                                  start=True, stop=True)
                    last.then_inc(s_qk, 1)

                def head(h, more):
                    b0 = l * 32 + h * 8
                    g0 = l * 48 + h * 12

                    def turned(b, g):
                        if g == 0:
                            pe.wait_ge(s_ad, b0 + b + 1)
                        pe.wait_ge(s_ate, 1 + g0 + groups_before(b) + g)
                        for t in range(4 * g, min(4 * g + 4, b + 1)):
                            o = Fp + 2048 * (b % 2) + P * t
                            last = nc.tensor.transpose(ps[:, 6, t % 4 * P:t % 4 * P + P],
                                                       F[:, o:o + P], ident)
                        last.then_inc(s_at, 1)

                    def weighted(b):
                        pe.wait_ge(s_on, 1 + b0 + b)
                        pe.wait_ge(s_ate, 1 + g0 + groups_before(b + 1))
                        for t in range(b + 1):
                            last = mm(ps[:, 7, 0:DV], F[:, Fat + P * t:Fat + P * t + P],
                                      F[:, bass.ds(h * DV + (Fv + 512 * t), DV)],
                                      start=(t == 0), stop=(t == b))
                        last.then_inc(s_pv, 1)

                    for b in range(NT):
                        if 2 * b + 3 < 2 * NT:
                            scores(h, 2 * b + 3)
                        if b:
                            weighted(b - 1)
                        turned(b, 0)
                        if 2 * b + 4 < 2 * NT:
                            scores(h, 2 * b + 4)
                        elif b == NT - 1 and more:
                            pe.wait_ge(s_q, l * HEADS + h + 2)
                            scores(h + 1, 0)
                            scores(h + 1, 1)
                        if b >= 4:
                            turned(b, 1)
                    if more:
                        scores(h + 1, 2)
                    weighted(NT - 1)

                pe.wait_ge(s_q, l * HEADS + 1)
                for u in range(3):
                    scores(0, u)
                apart(pe)
                with pe.Fori(0, HEADS - 1) as h:
                    head(h, True)
                head(HEADS - 1, False)
                def gate_row(s):
                    pe.wait_ge(s_dg, l * 2 + s + 1)
                    for k in range(KT):
                        last = mm(pair(0)[:, k * P:k * P + P], ones[:], diag[:, k, :],
                                  start=True, stop=True)
                    last.then_inc(s_gbp, 1)

                pe.wait_ge(s_ex, 1 + l * 64 + 64)
                gate_row(0)
                for h in range(HEADS):
                    pe.wait_ge(s_ov, l * HEADS + h + 1)
                    to_features(HEADS + h, lambda t: F[:, Fg + S * h + DV * t:Fg + S * h + DV * t + DV])

                def down(hs, r, first, last_k, free):
                    for i in range(4):
                        if first:
                            free(i)
                        for z, zz in ((0, 0), (0, 1), (1, 0)):
                            for c in range(2):
                                last = mm(pair(i)[:, 512 * c:512 * c + 512], hs(z, i),
                                          wsp[:, r, zz, 512 * c:512 * c + 512],
                                          start=first and z == 0 and zz == 0,
                                          stop=last_k and z == 1)
                        if last_k and i < 3:
                            last.then_inc(s_y, 1)
                    last.then_inc(s_pe, 1)

                pe.wait_ge(s_gb, l * 2 + 1)
                pe.wait_ge(s_ol, 1 + l * 8 + 8)
                for g in range(2):
                    def free(i):
                        if g:
                            pe.wait_ge(s_yu, 1 + l * 16 + i + 1)
                    for k in range(KT):
                        n = N_OUT + g * KT + k
                        split(n)
                        down(lambda z, i: hT[:, z, k, (4 * g + i) * P:(4 * g + i + 1) * P], n % 2,
                             k == 0, k == KT - 1, free)
                for t in range(NT):
                    norm_tr(8, t)

                def first_gate_up(r):
                    def slot(hf):
                        split(N_FF + r)
                        return columns(r, r, (hf,))
                    return slot
                halves_in_turn(8, first_gate_up(0), first_gate_up(1))

                def gate_up(i, pairs):
                    for jj in pairs:
                        pe.wait_ge(s_f2, l * JT + i * 2 + (jj + 1))
                        for r in range(2):
                            pe.wait_ge(s_lo, l * SLOTS + i * 4 + (N_FF + 2 * jj + r + 1 + CREDIT))
                            columns(r, 2 * jj + r).then_inc(s_pe, 1)
                gate_up(0, (1,))
                with pe.Fori(1, JT // 2) as i:
                    gate_up(i, (0, 1))
                pe.wait_ge(s_mod, l * MODS + MODS)
                pe.wait_ge(s_f2, l * JT + JT - 1 + CREDIT)
                for q in range(MOD1):
                    last = mm(ps[:, 2, q:q + 1], next_sums[:, q * P:q * P + P], ones[:, 0:1],
                              start=True, stop=True)
                last.then_inc(s_ma, 1)
                pe.wait_ge(s_f2, l * JT + JT + CREDIT)
                gate_row(1)
                pe.wait_ge(s_gb, l * 2 + 2)
                pe.wait_ge(s_modv, l * 2 + 3)
                for g in range(2):
                    def free(i):
                        if g:
                            pe.wait_ge(s_yu, 1 + l * 16 + 8 + i + 1)

                    def acts(r):
                        return lambda z, i: hT[:, z, r, i * P:i * P + P]
                    for r in range(2):
                        n = N_DOWN + g * JT + r
                        split(n)
                        pe.wait_ge(s_al, 1 + l * (2 * JT) + g * JT + r + 1)
                        down(acts(r), r, r == 0, False, free)
                    with pe.Fori(1, JT // 2 - 1) as i:
                        for r in range(2):
                            pe.wait_ge(s_lo, l * SLOTS + i * 2 + (N_DOWN + g * JT + r + 1 + CREDIT))
                            pe.wait_ge(s_al, 1 + l * (2 * JT) + i * 2 + (g * JT + r + 1))
                            down(acts(r), r, False, False, free)
                    for r in range(2):
                        n = N_DOWN + g * JT + JT - 2 + r
                        split(n)
                        pe.wait_ge(s_al, 1 + l * (2 * JT) + g * JT + JT - 2 + r + 1)
                        down(acts(r), r, False, r == 1, free)


_INS = ["x", "c", "w_mod", "b_mod", "norm_gains", "w_in", "w_gla_gate", "b_gla_gate", "gla_norm",
        "diff_lambda", "diff_norm", "rel_bias", "w_out", "w_gate_up", "w_down"]


def kernel(**inputs):
    import concourse.bacc as bacc
    from concourse.bass_utils import run_bass_kernel_spmd

    nc = bacc.Bacc("TRN2", target_bir_lowering=False, num_devices=1)
    arrays, args = {}, []
    consts, hot = layer_constants()
    given = [(k, np.ascontiguousarray(inputs[k])) for k in _INS] + [("consts", consts), ("onehot", hot)]
    for name, a in given:
        if name == "x":
            a = a.reshape(S, D)
        arrays[f"in_{name}"] = a
        args.append(nc.dram_tensor(f"in_{name}", a.shape, F32, kind="ExternalInput").ap())
    args.append(nc.dram_tensor("bias_rows", (HEADS, P, 3 * P), F32, kind="Internal").ap())
    out = nc.dram_tensor("out_x", (S, D), F32, kind="ExternalOutput").ap()
    args.append(out)
    build(nc, *args)
    r = run_bass_kernel_spmd(nc, [arrays], core_ids=[0])
    return r.results[0]["out_x"].reshape(1, S, D)
```
